# Optimizing a Trainium2 kernel written in Bass

```python
import math
import jax, jax.numpy as jnp
from jax import lax
import numpy as np

D_MODEL = 1024
BATCH = 1
SEQ = 512
DEPTH = 1

GDN_HEADS = 4
GDN_HEAD_DIM = 128
GDN_WIDTH = GDN_HEADS * GDN_HEAD_DIM
CONV_WIDTH = 4
GDN_CHUNK = 64
DSA_HEADS = 4
DSA_HEAD_DIM = 128
DSA_WIDTH = DSA_HEADS * DSA_HEAD_DIM
Q_RANK = 256
KV_RANK = 256
IDX_HEADS = 16
IDX_DIM = 64
IDX_TOPK_MAX = 256
Q_BLOCK = 128
REL_BUCKETS = 32
REL_MAX_DIST = 1024
PEER_HEADS = 8
PEER_KEYS = 128
PEER_EXPERTS = PEER_KEYS * PEER_KEYS
PEER_KEY_DIM = 256
PEER_TOPK = 16
PEER_BLOCK = 128

MIX_WIDTH = GDN_WIDTH + DSA_WIDTH
IN_SPLIT_SIZES = (GDN_WIDTH, GDN_WIDTH, GDN_WIDTH, GDN_WIDTH, GDN_HEADS, GDN_HEADS,
                  Q_RANK, KV_RANK, IDX_DIM, IDX_HEADS)
IN_WIDTH = sum(IN_SPLIT_SIZES)
EPS = 1e-6
F32 = jnp.float32

kernel_name = "hybrid_gdn_dsa_peer_block"

def rms_norm(x, g):
    xf = x.astype(F32)
    y = xf * lax.rsqrt(jnp.mean(xf * xf, axis=-1, keepdims=True) + EPS)
    return (y * g.astype(F32)).astype(x.dtype)

def layer_norm(x, g, b):
    xf = x.astype(F32)
    mu = jnp.mean(xf, axis=-1, keepdims=True)
    xc = xf - mu
    y = xc * lax.rsqrt(jnp.mean(xc * xc, axis=-1, keepdims=True) + EPS)
    return (y * g.astype(F32) + b.astype(F32)).astype(x.dtype)

def l2_normalize(x):
    xf = x.astype(F32)
    return xf * lax.rsqrt(jnp.sum(xf * xf, axis=-1, keepdims=True) + EPS)

def causal_depthwise_conv(x, w):
    c = x.shape[-1]
    return lax.conv_general_dilated(
        x, w[:, None, :].astype(x.dtype), window_strides=(1,),
        padding=((CONV_WIDTH - 1, 0),), dimension_numbers=('NWC', 'WIO', 'NWC'),
        feature_group_count=c)

def gated_delta_rule(q, k, v, g, beta):
    bsz, t_len, h, dk = q.shape
    dv = v.shape[-1]
    c = GDN_CHUNK
    n = t_len // c
    q = q.astype(F32) * (dk ** -0.5)

    def chunk4(a):
        return a.astype(F32).reshape(bsz, n, c, h, a.shape[-1]).transpose(0, 3, 1, 2, 4)

    def chunk3(a):
        return a.astype(F32).reshape(bsz, n, c, h).transpose(0, 3, 1, 2)

    q, k, v = chunk4(q), chunk4(k), chunk4(v)
    g = jnp.cumsum(chunk3(g), axis=-1)
    beta = chunk3(beta)
    tril = jnp.tril(jnp.ones((c, c), dtype=bool))
    strict = jnp.tril(jnp.ones((c, c), dtype=bool), -1)
    decay = jnp.exp(jnp.where(tril, g[..., :, None] - g[..., None, :], -jnp.inf))
    k_beta = k * beta[..., None]
    v_beta = v * beta[..., None]
    a_mat = jnp.where(strict, jnp.einsum('bhncd,bhnsd->bhncs', k_beta, k) * decay, 0.0)
    eye = jnp.eye(c, dtype=F32)
    t_inv = lax.linalg.triangular_solve(a_mat + eye, jnp.broadcast_to(eye, a_mat.shape),
                                        left_side=True, lower=True, unit_diagonal=True)
    u = jnp.einsum('bhncs,bhnse->bhnce', t_inv, v_beta)
    w = jnp.einsum('bhncs,bhnsd->bhncd', t_inv, k_beta * jnp.exp(g)[..., None])
    attn = jnp.einsum('bhncd,bhnsd->bhncs', q, k) * decay

    def step(state, xs):
        q_c, k_c, u_c, w_c, g_c, a_c = xs
        v_new = u_c - jnp.einsum('bhcd,bhde->bhce', w_c, state)
        o_c = (jnp.einsum('bhcd,bhde->bhce', q_c * jnp.exp(g_c)[..., None], state)
               + jnp.einsum('bhcs,bhse->bhce', a_c, v_new))
        g_last = g_c[..., -1:]
        state = (state * jnp.exp(g_last)[..., None]
                 + jnp.einsum('bhcd,bhce->bhde', k_c * jnp.exp(g_last - g_c)[..., None], v_new))
        return state, o_c

    xs = (q.transpose(2, 0, 1, 3, 4), k.transpose(2, 0, 1, 3, 4), u.transpose(2, 0, 1, 3, 4),
          w.transpose(2, 0, 1, 3, 4), g.transpose(2, 0, 1, 3), attn.transpose(2, 0, 1, 3, 4))
    s0 = jnp.zeros((bsz, h, dk, dv), F32)
    _, o = lax.scan(step, s0, xs)
    return o.transpose(1, 0, 3, 2, 4).reshape(bsz, t_len, h, dv)

def gdn_mixer(q, k, v, z, a, b, conv_w, a_log, dt_bias, norm_g):
    bsz, t_len, _ = q.shape
    qkv = jax.nn.silu(causal_depthwise_conv(jnp.concatenate([q, k, v], axis=-1), conv_w))
    q, k, v = jnp.split(qkv, [GDN_WIDTH, 2 * GDN_WIDTH], axis=-1)
    q = l2_normalize(q.reshape(bsz, t_len, GDN_HEADS, GDN_HEAD_DIM))
    k = l2_normalize(k.reshape(bsz, t_len, GDN_HEADS, GDN_HEAD_DIM))
    v = v.reshape(bsz, t_len, GDN_HEADS, GDN_HEAD_DIM)
    g = -jnp.exp(a_log.astype(F32)) * jax.nn.softplus(a.astype(F32) + dt_bias.astype(F32))
    beta = jax.nn.sigmoid(b.astype(F32))
    o = gated_delta_rule(q, k, v, g, beta)
    o = rms_norm(o, norm_g) * jax.nn.silu(z.reshape(bsz, t_len, GDN_HEADS, GDN_HEAD_DIM).astype(F32))
    return o.reshape(bsz, t_len, GDN_WIDTH).astype(z.dtype)

def rel_bucket(dist):
    max_exact = REL_BUCKETS // 2
    n = jnp.maximum(dist, 0)
    nf = jnp.maximum(n, 1).astype(F32)
    large = max_exact + (jnp.log(nf / max_exact) / math.log(REL_MAX_DIST / max_exact)
                         * (REL_BUCKETS - max_exact)).astype(jnp.int32)
    large = jnp.minimum(large, REL_BUCKETS - 1)
    return jnp.where(n < max_exact, n, large)

def dsa_mixer(c_q, c_kv, k_idx, w_idx, q_norm_g, kv_norm_g, w_q_up, w_qidx_up, w_kv_up,
              idx_ln_g, idx_ln_b, rel_bias):
    bsz, t_len, _ = c_q.shape
    cq = rms_norm(c_q, q_norm_g)
    q = (cq @ w_q_up).reshape(bsz, t_len, DSA_HEADS, DSA_HEAD_DIM)
    q_idx = (cq @ w_qidx_up).reshape(bsz, t_len, IDX_HEADS, IDX_DIM)
    ckv = rms_norm(c_kv, kv_norm_g)
    kv = (ckv @ w_kv_up).reshape(bsz, t_len, DSA_HEADS, 2 * DSA_HEAD_DIM)
    k, v = kv[..., :DSA_HEAD_DIM], kv[..., DSA_HEAD_DIM:]
    k_idx = layer_norm(k_idx, idx_ln_g, idx_ln_b).astype(F32)
    w_idx = w_idx.astype(F32) * (IDX_HEADS ** -0.5 * IDX_DIM ** -0.5)
    topk = min(IDX_TOPK_MAX, t_len // 4)
    nb = t_len // Q_BLOCK
    scale = DSA_HEAD_DIM ** -0.5
    key_pos = jnp.arange(t_len)

    def blk(a):
        return a.reshape(bsz, nb, Q_BLOCK, *a.shape[2:]).swapaxes(0, 1)

    def attend_block(args):
        i, q_b, qi_b, wi_b = args
        t_pos = i * Q_BLOCK + jnp.arange(Q_BLOCK)
        causal = key_pos[None, :] <= t_pos[:, None]
        idx_logits = jnp.einsum('bthd,bsd->bths', qi_b.astype(F32), k_idx)
        score = jnp.einsum('bths,bth->bts', jax.nn.relu(idx_logits), wi_b)
        score = jnp.where(causal[None], score, -jnp.inf)
        _, sel = lax.top_k(score, topk)
        k_sel = jax.vmap(lambda kk, ii: kk[ii])(k, sel)
        v_sel = jax.vmap(lambda vv, ii: vv[ii])(v, sel)
        logits = jnp.einsum('bthd,btkhd->bhtk', q_b.astype(F32), k_sel.astype(F32)) * scale
        dist = t_pos[None, :, None] - sel
        bias = rel_bias[rel_bucket(dist)].astype(F32)
        logits = logits + bias.transpose(0, 3, 1, 2)
        logits = jnp.where((dist >= 0)[:, None], logits, -jnp.inf)
        p = jax.nn.softmax(logits, axis=-1)
        out = jnp.einsum('bhtk,btkhd->bthd', p, v_sel.astype(F32))
        return out.astype(q_b.dtype)

    outs = lax.map(attend_block, (jnp.arange(nb), blk(q), blk(q_idx), blk(w_idx)))
    return outs.swapaxes(0, 1).reshape(bsz, t_len, DSA_WIDTH)

def peer_ffn(h, w_query, sub_keys_1, sub_keys_2, expert_u, expert_v):
    bsz, t_len, d = h.shape
    nb = t_len // PEER_BLOCK
    n_tok = bsz * PEER_BLOCK
    half = PEER_KEY_DIM // 2
    hb = h.reshape(bsz, nb, PEER_BLOCK, d).swapaxes(0, 1).reshape(nb, n_tok, d)

    def block(xb):
        qy = (xb @ w_query).reshape(n_tok, PEER_HEADS, 2, half)
        s1 = jnp.einsum('nhd,hkd->nhk', qy[:, :, 0], sub_keys_1).astype(F32)
        s2 = jnp.einsum('nhd,hkd->nhk', qy[:, :, 1], sub_keys_2).astype(F32)
        v1, i1 = lax.top_k(s1, PEER_TOPK)
        v2, i2 = lax.top_k(s2, PEER_TOPK)
        cand = (v1[..., :, None] + v2[..., None, :]).reshape(n_tok, PEER_HEADS, PEER_TOPK * PEER_TOPK)
        cidx = (i1[..., :, None] * PEER_KEYS + i2[..., None, :]).reshape(n_tok, PEER_HEADS, PEER_TOPK * PEER_TOPK)
        top_s, pos = lax.top_k(cand, PEER_TOPK)
        eidx = jnp.take_along_axis(cidx, pos, axis=-1)
        gates = jax.nn.softmax(top_s, axis=-1)
        u = expert_u[eidx]
        vv = expert_v[eidx]
        act = jax.nn.gelu(jnp.einsum('nhkd,nd->nhk', u, xb).astype(F32), approximate=False)
        return jnp.einsum('nhk,nhkd->nd', (gates * act).astype(vv.dtype), vv)

    y = lax.map(block, hb)
    return y.reshape(nb, bsz, PEER_BLOCK, d).swapaxes(0, 1).reshape(bsz, t_len, d)

def setup_inputs(seed: int = 0) -> dict:
    key = jax.random.key(seed)
    ks = jax.random.split(key, 24)
    nrm = lambda k, shape, s: jax.random.normal(k, shape, F32) * s
    gain = lambda k, shape: 1.0 + 0.02 * jax.random.normal(k, shape, F32)
    dt = jnp.exp(jax.random.uniform(ks[4], (DEPTH, GDN_HEADS), F32, math.log(1e-3), math.log(1e-1)))
    return {
        "x": nrm(ks[0], (BATCH, SEQ, D_MODEL), 1.0),
        "ln1_g": gain(ks[1], (DEPTH, D_MODEL)),
        "w_in": nrm(ks[2], (DEPTH, D_MODEL, IN_WIDTH), D_MODEL ** -0.5),
        "conv_w": nrm(ks[3], (DEPTH, CONV_WIDTH, 3 * GDN_WIDTH), CONV_WIDTH ** -0.5),
        "a_log": jnp.log(jax.random.uniform(ks[5], (DEPTH, GDN_HEADS), F32, 1.0, 16.0)),
        "dt_bias": dt + jnp.log(-jnp.expm1(-dt)),
        "gdn_norm_g": gain(ks[6], (DEPTH, GDN_HEAD_DIM)),
        "q_norm_g": gain(ks[7], (DEPTH, Q_RANK)),
        "kv_norm_g": gain(ks[8], (DEPTH, KV_RANK)),
        "w_q_up": nrm(ks[9], (DEPTH, Q_RANK, DSA_WIDTH), Q_RANK ** -0.5),
        "w_qidx_up": nrm(ks[10], (DEPTH, Q_RANK, IDX_HEADS * IDX_DIM), Q_RANK ** -0.5),
        "w_kv_up": nrm(ks[11], (DEPTH, KV_RANK, 2 * DSA_WIDTH), KV_RANK ** -0.5),
        "idx_ln_g": gain(ks[12], (DEPTH, IDX_DIM)),
        "idx_ln_b": nrm(ks[13], (DEPTH, IDX_DIM), 0.02),
        "w_out": nrm(ks[14], (DEPTH, MIX_WIDTH, D_MODEL), MIX_WIDTH ** -0.5),
        "ln2_g": gain(ks[15], (DEPTH, D_MODEL)),
        "peer_w_query": nrm(ks[16], (DEPTH, D_MODEL, PEER_HEADS * PEER_KEY_DIM), D_MODEL ** -0.5),
        "peer_sub_keys_1": nrm(ks[17], (DEPTH, PEER_HEADS, PEER_KEYS, PEER_KEY_DIM // 2), (PEER_KEY_DIM // 2) ** -0.5),
        "peer_sub_keys_2": nrm(ks[18], (DEPTH, PEER_HEADS, PEER_KEYS, PEER_KEY_DIM // 2), (PEER_KEY_DIM // 2) ** -0.5),
        "peer_u": nrm(ks[19], (DEPTH, PEER_EXPERTS, D_MODEL), D_MODEL ** -0.5),
        "peer_v": nrm(ks[20], (DEPTH, PEER_EXPERTS, D_MODEL), PEER_HEADS ** -0.5),
        "rel_bias": nrm(ks[21], (REL_BUCKETS, DSA_HEADS), 0.5),
        "final_g": gain(ks[22], (D_MODEL,)),
    }

def reference(x, ln1_g, w_in, conv_w, a_log, dt_bias, gdn_norm_g, q_norm_g, kv_norm_g,
              w_q_up, w_qidx_up, w_kv_up, idx_ln_g, idx_ln_b, w_out, ln2_g, peer_w_query,
              peer_sub_keys_1, peer_sub_keys_2, peer_u, peer_v, rel_bias, final_g):
    offsets = [int(o) for o in np.cumsum(IN_SPLIT_SIZES)[:-1]]
    for l in range(DEPTH):
        h = rms_norm(x, ln1_g[l])
        proj = h @ w_in[l]
        gq, gk, gv, gz, ga, gb, cq, ckv, kidx, widx = jnp.split(proj, offsets, axis=-1)
        o_a = gdn_mixer(gq, gk, gv, gz, ga, gb, conv_w[l], a_log[l], dt_bias[l], gdn_norm_g[l])
        o_b = dsa_mixer(cq, ckv, kidx, widx, q_norm_g[l], kv_norm_g[l], w_q_up[l], w_qidx_up[l],
                        w_kv_up[l], idx_ln_g[l], idx_ln_b[l], rel_bias)
        x = x + jnp.concatenate([o_a, o_b], axis=-1) @ w_out[l]
        x = x + peer_ffn(rms_norm(x, ln2_g[l]), peer_w_query[l], peer_sub_keys_1[l],
                         peer_sub_keys_2[l], peer_u[l], peer_v[l])
    return rms_norm(x, final_g)


_drawn_inputs = setup_inputs


def setup_inputs(seed=0):
    import zlib

    import numpy as np

    out = dict(_drawn_inputs(seed))
    spreads = {}
    factors = {'gdn_norm_g': 21.178,
     'q_norm_g': 3.041,
     'kv_norm_g': 5.239,
     'idx_ln_g': 3.426,
     'idx_ln_b': 3.719,
     'final_g': 7.969,
     'ln2_g': 7.972}
    for name, (base, spread) in spreads.items():
        noise = np.random.default_rng([zlib.crc32(name.encode()), seed]).standard_normal(out[name].shape)
        drawn = base * np.exp(spread * noise) if base else spread * noise
        out[name] = __import__('jax').numpy.asarray(drawn.astype(out[name].dtype))
    for name, factor in factors.items():
        out[name] = (out[name] * factor).astype(out[name].dtype)
    return out
```

```python
from contextlib import ExitStack
import math

import numpy as np
import concourse.bass as bass
from concourse import mybir

F32 = mybir.dt.float32
F32R = mybir.dt.float32r
U32 = mybir.dt.uint32
ACT = mybir.ActivationFunctionType
ALU = mybir.AluOpType
AX = mybir.AxisListType

P = 128
T = 512
NB = T // P
D = 1024
DC = D // P
H = 4
CONV = 4
CHUNK = 64
NCH = T // CHUNK
RANK = 256
IH, IDIM = 16, 64
TOPK = 128
BUCKETS = 32
PH, PK, PTOP = 8, 128, 16
CH = 64
EPS = 1e-6
PAD = CONV - 1

QKV_T = 3 * H
Z0, CQ0, CKV0, KI0, AB0 = 12, 16, 18, 20, 21
NPROJ = 22
NEG = -1e30
TAKEN = -3.0e38
OUT_OF_REACH = -2.0e38

C_ID, C_ONES, C_CUM, C_STRICT, C_SAME, C_HALF0, C_ANTI, C_IOTA, C_M0, C_MT = 0, 1, 2, 3, 4, 5, 7, 8, 9, 10
LEVELS = 6
C_N = C_MT + LEVELS
V_LN1, V_LN2, V_FIN, V_CONV, V_GDN, V_QN, V_KVN, V_IG, V_IB, V_EPS, V_ALOG, V_DTB, V_N = (
    0, 8, 16, 24, 72, 73, 75, 77, 78, 79, 80, 84, 88)


def constants():
    r, c = np.arange(P)[:, None], np.arange(P)[None, :]
    same = r // CHUNK == c // CHUNK
    t = np.zeros((P, C_N, P), np.float32)
    t[:, C_ID] = r == c
    t[:, C_ONES] = 1
    t[:, C_CUM] = same & (r <= c)
    t[:, C_STRICT] = same & (c < r)
    t[:, C_SAME] = same
    t[:, C_HALF0] = (r < CHUNK) & (c >= 0)
    t[:, C_HALF0 + 1] = (r >= CHUNK) & (c >= 0)
    t[:, C_ANTI] = r + c == P - 1
    t[:, C_IOTA] = c + 0 * r
    for level in range(LEVELS):
        w = 1 << level
        low = (r // (2 * w) == c // (2 * w)) & (r // w % 2 == 1) & (c // w % 2 == 0)
        if level == 0:
            t[:, C_M0] = low
        t[:, C_MT + level] = low.T
    return t.reshape(P, C_N * P)


def bucket_rows():
    dist = T - 1 - np.arange(T + P)
    n = np.maximum(dist, 0)
    exact = BUCKETS // 2
    nf = np.maximum(n, 1).astype(np.float32)
    large = exact + (np.log(nf / np.float32(exact)) / np.float32(math.log(1024 / exact))
                     * np.float32(BUCKETS - exact)).astype(np.int32)
    b = np.where(n < exact, n, np.minimum(large, BUCKETS - 1))
    return (b[None, :] == np.arange(BUCKETS)[:, None]).astype(np.float32)


class Tables:

    def __init__(self, nc, outer):
        self.nc = nc
        self.held = []
        self.bank = [outer.enter_context(nc.psum_tensor(f"bank{i}", [P, T], F32)) for i in range(8)]
        self.cst = outer.enter_context(nc.sbuf_tensor("cst", [P, C_N * P], F32))
        self.vec = outer.enter_context(nc.sbuf_tensor("vec", [P, V_N], F32))

    def sem(self, name):
        self.held.append(self.nc.alloc_semaphore(name=name))
        return self.held[-1]

    def free_semaphores(self):
        self.nc.clear_and_free_semaphores(self.held)
        self.nc.all_engine_barrier()
        self.held = []

    def c(self, k, n=1):
        return self.cst[:, k * P:(k + n) * P]

    def per_block(self, k):
        return self.cst[:, k * P:(k + 1) * P].unsqueeze(1).to_broadcast([P, NB, P])


def blocks(ap):
    return ap.rearrange("p (b c) -> p b c", b=NB)


def load_stage(t, x_d, cst_d, vec_d, x):
    nc = t.nc
    loaded = t.sem("loaded")
    with nc.Block() as block:

        @block.sync
        def _(sp):
            sp.dma_start(x[:], x_d).then_inc(loaded, 16)
            sp.dma_start(t.cst[:], cst_d).then_inc(loaded, 16)
            sp.dma_start(t.vec[:], vec_d).then_inc(loaded, 16)
            sp.wait_ge(loaded, 48)


def norm_stage(t, tag, x, gain, hi=None, lo=None, out=None):
    nc = t.nc
    squared, summed, rooted = (t.sem(f"{tag}_{n}") for n in ("squared", "summed", "rooted"))
    inverted, normed, high, low = (t.sem(f"{tag}_{n}") for n in ("inverted", "normed", "high", "low"))
    with ExitStack() as ctx:
        sq = ctx.enter_context(nc.sbuf_tensor(f"{tag}_sq", [P, DC, T], F32))
        root = ctx.enter_context(nc.sbuf_tensor(f"{tag}_root", [P, T], F32))
        inv = ctx.enter_context(nc.sbuf_tensor(f"{tag}_inv", [P, T], F32))
        y = out if out is not None else sq
        with nc.Block() as block:

            @block.scalar
            def _(act):
                for c in range(DC):
                    nc.scalar.activation(sq[:, c, :], x[:, c, :], ACT.Square).then_inc(squared, 1)
                act.wait_ge(summed, 1)
                nc.scalar.activation(root[:], t.bank[0][:], ACT.Sqrt, scale=1.0 / D,
                                     bias=t.vec[:, V_EPS:V_EPS + 1]).then_inc(rooted, 1)
                if hi is not None:
                    for c in range(DC):
                        act.wait_ge(normed, c + 1)
                        nc.scalar.activation(hi[:, c, :], y[:, c, :], ACT.Copy).then_inc(high, 1)

            @block.tensor
            def _(pe):
                for c in range(DC):
                    pe.wait_ge(squared, c + 1)
                    last = nc.tensor.matmul(t.bank[0][:], t.c(C_ONES), sq[:, c, :],
                                            start=c == 0, stop=c == DC - 1)
                last.then_inc(summed, 1)

            @block.vector
            def _(dve):
                dve.wait_ge(rooted, 1)
                nc.vector.reciprocal(inv[:], root[:]).then_inc(inverted, 1)
                dve.wait_ge(inverted, 1)
                for c in range(DC):
                    nc.vector.scalar_tensor_tensor(y[:, c, :], x[:, c, :], t.vec[:, gain + c:gain + c + 1],
                                                   inv[:], ALU.mult, ALU.mult).then_inc(normed, 1)
                if hi is not None:
                    for c in range(DC):
                        dve.wait_ge(high, c + 1)
                        nc.vector.tensor_tensor(lo[:, c, :], y[:, c, :], hi[:, c, :].bitcast(F32),
                                                ALU.subtract).then_inc(low, 1)


def project_stage(t, tag, w_d, n, hi, lo, dest, add=None):
    nc = t.nc
    loaded = [t.sem(f"{tag}_loaded{s}") for s in range(2)]
    w_high, w_low, summed, stored = (t.sem(f"{tag}_{k}") for k in ("w_high", "w_low", "summed", "stored"))
    with ExitStack() as ctx:
        raw = ctx.enter_context(nc.sbuf_tensor(f"{tag}_raw", [P, 2, D], F32))
        whi = ctx.enter_context(nc.sbuf_tensor(f"{tag}_whi", [P, 2, D], F32R))
        wlo = ctx.enter_context(nc.sbuf_tensor(f"{tag}_wlo", [P, 2, D], F32R))
        with nc.Block() as block:

            @block.sync
            def _(sp):
                def load(i, first):
                    for s in range(2):
                        if not first:
                            sp.wait_ge(w_low, 2 * i + s - 1)
                        sp.dma_start(raw[:, s, :], w_d[2 * i + s]).then_inc(loaded[s], 16)
                load(0, True)
                with sp.Fori(1, n // 2) as i:
                    load(i, False)

            @block.scalar
            def _(act):
                def high(i, s, first):
                    act.wait_ge(loaded[s], 16 * (i + 1))
                    if not first:
                        act.wait_ge(summed, 2 * i + s - 1)
                    nc.scalar.activation(whi[:, s, :], raw[:, s, :], ACT.Copy).then_inc(w_high, 1)

                def store(i, s):
                    act.wait_ge(summed, 2 * i + s + 1)
                    nc.scalar.activation(dest(2 * i + s), t.bank[s][:], ACT.Copy).then_inc(stored, 1)

                high(0, 0, True)
                high(0, 1, True)
                if add is None:
                    store(0, 0)
                with act.Fori(1, n // 2) as i:
                    high(i, 0, False)
                    if add is None:
                        store(i - 1, 1)
                    high(i, 1, False)
                    if add is None:
                        store(i, 0)
                if add is None:
                    store(n // 2 - 1, 1)

            @block.vector
            def _(dve):
                def low(i, s):
                    dve.wait_ge(w_high, 2 * i + s + 1)
                    nc.vector.tensor_tensor(wlo[:, s, :], raw[:, s, :], whi[:, s, :].bitcast(F32),
                                            ALU.subtract).then_inc(w_low, 1)

                def store(i, s):
                    dve.wait_ge(summed, 2 * i + s + 1)
                    nc.vector.tensor_tensor(dest(2 * i + s), add(2 * i + s), t.bank[s][:],
                                            ALU.add).then_inc(stored, 1)

                low(0, 0)
                low(0, 1)
                if add is not None:
                    store(0, 0)
                with dve.Fori(1, n // 2) as i:
                    low(i, 0)
                    if add is not None:
                        store(i - 1, 1)
                    low(i, 1)
                    if add is not None:
                        store(i, 0)
                if add is not None:
                    store(n // 2 - 1, 1)

            @block.tensor
            def _(pe):
                def product(i, first):
                    for s in range(2):
                        pe.wait_ge(w_low, 2 * i + s + 1)
                        if not first:
                            pe.wait_ge(stored, 2 * i + s - 1)
                        for c in range(DC):
                            w = slice(c * P, (c + 1) * P)
                            nc.tensor.matmul(t.bank[s][:], whi[:, s, w], hi[:, c, :], start=c == 0, stop=False)
                            nc.tensor.matmul(t.bank[s][:], whi[:, s, w], lo[:, c, :], start=False, stop=False)
                            last = nc.tensor.matmul(t.bank[s][:], wlo[:, s, w], hi[:, c, :], start=False,
                                                    stop=c == DC - 1)
                        last.then_inc(summed, 1)
                product(0, True)
                with pe.Fori(1, n // 2) as i:
                    product(i, False)


def delta_stage(t, proj, mix):
    nc = t.nc
    s = {n: t.sem("gdn_" + n) for n in (
        "chain", "conv", "silu", "squared", "sumsq", "root", "normed", "ab_t", "ab", "exps", "u1", "log",
        "g", "beta", "cums", "g_col", "decays", "beg", "gl", "grow", "dif", "exp3", "dmask", "tiles_t", "kk",
        "kv_use", "a", "a_t", "at", "prep", "mt", "x", "xs", "tx", "level", "uw_t", "u", "w", "zero",
        "ws", "vnew", "out", "o_copy", "ds", "state", "osq", "ossq", "oroot", "zs", "zx", "mixed")}
    v = t.vec
    with ExitStack() as ctx:
        def sb(name, shape):
            return ctx.enter_context(nc.sbuf_tensor("gdn_" + name, shape, F32))

        conv = sb("conv", [P, 3 * H, T])
        qk = sb("qk", [P, 2 * H, T])
        sq = sb("sq", [P, 2 * H, T])
        ab = sb("ab", [P, NB, 8])
        small = sb("small", [P, 16, 16])
        ghalf = sb("ghalf", [P, 2, 16])
        qeg = sb("qeg", [P, H, T])
        at = sb("at", [P, H, T])
        attn = sb("attn", [P, H, T])
        mt_u = sb("mt_u", [P, H, T])
        x_w = sb("x_w", [P, H, T])
        tmp = sb("tmp", [P, 8, T])
        kbg, kdec, vb = conv[:, 0:H], conv[:, H:2 * H], conv[:, 2 * H:3 * H]
        ti, tt = sq[:, 0:H], sq[:, H:2 * H]
        gl, dif, pos, neg, eg, dn, dt, am = (tmp[:, i, :] for i in range(8))
        root = tmp[:, 0:2, :]
        sm = [small[:, i, :] for i in range(16)]
        xa, nx, z, u1, lnu, eq, rat, sp_, g, ebb, beta, gcol, eg_col, egam, beg, ea = sm

        def by_block(ap):
            return lambda h: ap.rearrange("p (b h) -> p b h", h=H)[:, :, h:h + 1].to_broadcast([P, NB, P])

        with nc.Block() as block:

            @block.vector
            def _(dve):
                chain = [0]

                def link(ins):
                    chain[0] += 1
                    ins.then_inc(s["chain"], 1)
                    dve.wait_ge(s["chain"], chain[0])

                tt_, ts = nc.vector.tensor_tensor, nc.vector.tensor_scalar
                stt = nc.vector.scalar_tensor_tensor
                dve.wait_ge(s["ab_t"], 1)
                link(nc.vector.tensor_copy(ab[:], blocks(t.bank[7][:])[:, :, 0:8]))
                r3 = lambda ap: ap.rearrange("p (b h) -> p b h", h=H)
                link(tt_(r3(xa), ab[:, :, 0:H], v[:, V_DTB:V_DTB + H].unsqueeze(1).to_broadcast([P, NB, H]), ALU.add))
                link(ts(nx, xa, -1.0, None, ALU.mult))
                tt_(nx, nx, xa, ALU.min).then_inc(s["ab"], 1)
                for j in range(3 * H):
                    def tap(k):
                        return v[:, V_CONV + j * CONV + k:V_CONV + j * CONV + k + 1]
                    link(ts(conv[:, j, :], proj[:, j, 0:T], tap(0), None, ALU.mult))
                    for k in range(1, CONV):
                        ins = stt(conv[:, j, :], proj[:, j, k:k + T], tap(k), conv[:, j, :], ALU.mult, ALU.add)
                        if k < CONV - 1:
                            link(ins)
                    ins.then_inc(s["conv"], 1)
                dve.wait_ge(s["exps"], 3)
                ts(u1, z, 1.0, None, ALU.add).then_inc(s["u1"], 1)
                dve.wait_ge(s["u1"], 1)
                link(ts(eq, u1, 1.0, None, ALU.is_equal))
                link(stt(rat, u1, -1.0, eq, ALU.add, ALU.add))
                link(nc.vector.reciprocal(rat, rat))
                link(tt_(rat, rat, z, ALU.mult))
                dve.wait_ge(s["log"], 1)
                link(tt_(lnu, lnu, eq, ALU.add))
                link(tt_(rat, rat, lnu, ALU.mult))
                link(stt(sp_, xa, 0.0, rat, ALU.max, ALU.add))
                tt_(r3(g), r3(sp_), ea[:, 0:H].unsqueeze(1).to_broadcast([P, NB, H]), ALU.mult).then_inc(s["chain"], 1)
                chain[0] += 1
                dve.wait_ge(s["chain"], chain[0])
                ts(g, g, -1.0, None, ALU.mult).then_inc(s["g"], 1)
                link(ts(beta, ebb, 1.0, None, ALU.add))
                nc.vector.reciprocal(beta, beta).then_inc(s["beta"], 1)
                dve.wait_ge(s["cums"], 1)
                nc.vector.tensor_copy(gcol, t.bank[6][:, 0:16]).then_inc(s["g_col"], 1)
                dve.wait_ge(s["g_col"], 1)
                link(tt_(egam, t.bank[6][:, 16:32], gcol, ALU.subtract))
                nc.vector.tensor_copy(ghalf[:], t.bank[6][:, 32:64].rearrange("p (a b) -> p a b", a=2)).then_inc(s["g_col"], 1)
                dve.wait_ge(s["decays"], 3)
                tt_(beg, beta, eg_col, ALU.mult).then_inc(s["beg"], 1)
                dve.wait_ge(s["beg"], 1)
                for j in range(2 * H):
                    dve.wait_ge(s["root"], j + 1)
                    link(nc.vector.reciprocal(root[:, j % 2, :], root[:, j % 2, :]))
                    stt(qk[:, j, :], conv[:, j, :], float(P) ** -0.5 if j < H else 1.0, root[:, j % 2, :],
                        ALU.mult, ALU.mult).then_inc(s["normed"], 1)
                dve.wait_ge(s["normed"], 2 * H)
                for h in range(H):
                    tt_(blocks(gl), t.per_block(C_CUM), by_block(g)(h), ALU.mult).then_inc(s["gl"], 1)
                    dve.wait_ge(s["grow"], h + 1)
                    link(tt_(blocks(dif), blocks(t.bank[0][:]), by_block(gcol)(h), ALU.subtract))
                    ts(pos, dif, 0.0, None, ALU.max).then_inc(s["dif"], 1)
                    ts(neg, dif, 0.0, None, ALU.min).then_inc(s["dif"], 1)
                    dve.wait_ge(s["exp3"], 3 * (h + 1))
                    tt_(qeg[:, h, :], qk[:, h, :], eg, ALU.mult)
                    link(tt_(blocks(dn), blocks(dn), t.per_block(C_STRICT), ALU.mult))
                    link(tt_(blocks(dn), blocks(dn), by_block(beta)(h), ALU.mult))
                    link(tt_(blocks(dt), blocks(dt), t.per_block(C_CUM), ALU.mult))
                    dve.wait_ge(s["tiles_t"], 2 * (h + 1))
                    tt_(blocks(kbg[:, h, :]), blocks(t.bank[1][:]), by_block(beg)(h), ALU.mult)
                    tt_(blocks(kdec[:, h, :]), blocks(t.bank[1][:]), by_block(egam)(h), ALU.mult)
                    tt_(blocks(vb[:, h, :]), blocks(t.bank[2][:]), by_block(beta)(h), ALU.mult)
                    dve.wait_ge(s["kk"], 2 * (h + 1))
                    tt_(am, t.bank[3][:], dn, ALU.mult).then_inc(s["a"], 1)
                    tt_(attn[:, h, :], t.bank[4][:], dt, ALU.mult)
                    dve.wait_ge(s["a"], h + 1)
                    link(tt_(blocks(ti[:, h, :]), blocks(am), t.per_block(C_M0), ALU.mult))
                    link(tt_(blocks(ti[:, h, :]), t.per_block(C_ID), blocks(ti[:, h, :]), ALU.subtract))
                    dve.wait_ge(s["at"], h + 1)
                    link(tt_(blocks(tt[:, h, :]), blocks(at[:, h, :]), t.per_block(C_MT), ALU.mult))
                    tt_(blocks(tt[:, h, :]), t.per_block(C_ID), blocks(tt[:, h, :]), ALU.subtract).then_inc(s["prep"], 1)
                dve.wait_ge(s["prep"], H)
                for level in range(1, LEVELS):
                    for h in range(H):
                        if level > 1:
                            dve.wait_ge(s["x"], H * (level - 2) + h + 1)
                        tt_(blocks(mt_u[:, h, :]), blocks(at[:, h, :]), t.per_block(C_MT + level),
                            ALU.mult).then_inc(s["mt"], 1)
                    for h in range(H):
                        dve.wait_ge(s["tx"], H * (level - 1) + h + 1)
                        if level < LEVELS - 1:
                            tt_(ti[:, h, :], ti[:, h, :], t.bank[4 + h % 2][:], ALU.subtract)
                        tt_(tt[:, h, :], tt[:, h, :], t.bank[6 + h % 2][:], ALU.subtract).then_inc(s["level"], 1)
                for h in range(H):
                    dve.wait_ge(s["uw_t"], h + 1)
                    nc.vector.tensor_copy(mt_u[:, h, :], t.bank[h % 2][:]).then_inc(s["u"], 1)
                states, vn, dec = (tmp[:, 0, :], tmp[:, 3, :]), tmp[:, 1, :], tmp[:, 2, :]
                nc.vector.memset(states[0], 0.0).then_inc(s["zero"], 1)
                dve.wait_ge(s["zero"], 1)
                dve.wait_ge(s["u"], H)
                u4 = mt_u[:].rearrange("p h (b c) -> p h b c", b=NB)
                for n in range(NCH):
                    b, rows = n // 2, slice(CHUNK * (n % 2), CHUNK * (n % 2) + CHUNK)
                    state, after = states[n % 2], states[(n + 1) % 2]
                    dve.wait_ge(s["ws"], n + 1)
                    tt_(vn[rows, :].rearrange("p (h c) -> p h c", h=H), u4[rows, :, b, :],
                        t.bank[4][rows, :].rearrange("p (h c) -> p h c", h=H), ALU.subtract).then_inc(s["vnew"], 1)
                    decay = ghalf[:, n % 2, b * H:(b + 1) * H].unsqueeze(2).to_broadcast([P, H, P])
                    link(tt_(dec.rearrange("p (h c) -> p h c", h=H), state.rearrange("p (h c) -> p h c", h=H),
                             decay, ALU.mult))
                    dve.wait_ge(s["ds"], n + 1)
                    tt_(after, dec, t.bank[6][:], ALU.add).then_inc(s["state"], 1)
                    dve.wait_ge(s["state"], n + 1)
                for h in range(H):
                    dve.wait_ge(s["oroot"], h + 1)
                    link(nc.vector.reciprocal(tmp[:, 4 + h % 2, :], tmp[:, 4 + h % 2, :]))
                    link(stt(qeg[:, h, :], qk[:, h, :], v[:, V_GDN:V_GDN + 1], tmp[:, 4 + h % 2, :], ALU.mult, ALU.mult))
                    dve.wait_ge(s["zs"], h + 1)
                    tt_(mix[:, h, :], qeg[:, h, :], attn[:, h, :], ALU.mult).then_inc(s["mixed"], 1)

            @block.scalar
            def _(act):
                a = nc.scalar.activation
                a(ea[:, 0:H], v[:, V_ALOG:V_ALOG + H], ACT.Exp).then_inc(s["exps"], 1)
                act.wait_ge(s["ab"], 1)
                a(z, nx, ACT.Exp).then_inc(s["exps"], 1)
                a(ebb.rearrange("p (b h) -> p b h", h=H), ab[:, :, H:2 * H], ACT.Exp, scale=-1.0).then_inc(s["exps"], 1)
                act.wait_ge(s["u1"], 1)
                a(lnu, u1, ACT.Ln).then_inc(s["log"], 1)
                for j in range(3 * H):
                    act.wait_ge(s["conv"], j + 1)
                    a(conv[:, j, :], conv[:, j, :], ACT.Silu).then_inc(s["silu"], 1)
                for j in range(2 * H):
                    act.wait_ge(s["silu"], j + 1)
                    a(sq[:, j, :], conv[:, j, :], ACT.Square).then_inc(s["squared"], 1)
                act.wait_ge(s["g_col"], 2)
                a(eg_col, gcol, ACT.Exp).then_inc(s["decays"], 1)
                a(egam, egam, ACT.Exp).then_inc(s["decays"], 1)
                a(ghalf[:], ghalf[:], ACT.Exp).then_inc(s["decays"], 1)
                for j in range(2 * H):
                    act.wait_ge(s["sumsq"], j + 1)
                    if j >= 2:
                        act.wait_ge(s["normed"], j - 1)
                    a(root[:, j % 2, :], t.bank[j % 2][:], ACT.Sqrt, bias=v[:, V_EPS:V_EPS + 1]).then_inc(s["root"], 1)
                for h in range(H):
                    act.wait_ge(s["dif"], 2 * h + 1)
                    if h:
                        act.wait_ge(s["prep"], h)
                    a(eg, t.bank[0][:], ACT.Exp).then_inc(s["exp3"], 1)
                    act.wait_ge(s["dif"], 2 * (h + 1))
                    a(dn, pos, ACT.Exp, scale=-1.0).then_inc(s["exp3"], 1)
                    a(dt, neg, ACT.Exp).then_inc(s["exp3"], 1)
                    act.wait_ge(s["a_t"], h + 1)
                    a(at[:, h, :], t.bank[5][:], ACT.Copy).then_inc(s["at"], 1)
                for level in range(1, LEVELS):
                    for h in range(H):
                        act.wait_ge(s["x"], H * (level - 1) + h + 1)
                        a(x_w[:, h, :], t.bank[h][:], ACT.Copy).then_inc(s["xs"], 1)
                for h in range(H):
                    act.wait_ge(s["uw_t"], h + 1)
                    a(x_w[:, h, :], t.bank[2 + h % 2][:], ACT.Copy).then_inc(s["w"], 1)
                for n in range(NCH):
                    act.wait_ge(s["out"], n + 1)
                    a(qk[:, 0:H, n * CHUNK:(n + 1) * CHUNK],
                      t.bank[5][:, 0:H * CHUNK].rearrange("p (h c) -> p h c", h=H), ACT.Copy).then_inc(s["o_copy"], 1)
                act.wait_ge(s["o_copy"], NCH)
                for h in range(H):
                    a(sq[:, h, :], qk[:, h, :], ACT.Square).then_inc(s["osq"], 1)
                for h in range(H):
                    a(attn[:, h, :], proj[:, Z0 + h, PAD:PAD + T], ACT.Silu).then_inc(s["zs"], 1)
                for h in range(H):
                    act.wait_ge(s["ossq"], h + 1)
                    if h >= 2:
                        act.wait_ge(s["mixed"], h - 1)
                    a(tmp[:, 4 + h % 2, :], t.bank[h % 2][:], ACT.Sqrt, scale=1.0 / P,
                      bias=v[:, V_EPS:V_EPS + 1]).then_inc(s["oroot"], 1)

            @block.tensor
            def _(pe):
                mm, tr = nc.tensor.matmul, nc.tensor.transpose
                ident, ones = t.c(C_ID), t.c(C_ONES)
                for b in range(NB):
                    last = tr(t.bank[7][:, b * P:(b + 1) * P], proj[:, AB0, PAD + b * P:PAD + (b + 1) * P], ident)
                last.then_inc(s["ab_t"], 1)
                pe.wait_ge(s["g"], 1)
                mm(t.bank[6][:, 0:16], t.c(C_CUM), g, start=True, stop=True)
                mm(t.bank[6][:, 16:32], t.c(C_SAME), g, start=True, stop=True)
                mm(t.bank[6][:, 32:48], t.c(C_HALF0), g, start=True, stop=True)
                mm(t.bank[6][:, 48:64], t.c(C_HALF0 + 1), g, start=True, stop=True).then_inc(s["cums"], 1)
                for j in range(2 * H):
                    pe.wait_ge(s["squared"], j + 1)
                    if j >= 2:
                        pe.wait_ge(s["root"], j - 1)
                    mm(t.bank[j % 2][:], ones, sq[:, j, :], start=True, stop=True).then_inc(s["sumsq"], 1)
                pe.wait_ge(s["silu"], 3 * H)
                for h in range(H):
                    pe.wait_ge(s["gl"], h + 1)
                    if h == 0:
                        pe.wait_ge(s["root"], 2 * H)
                    mm(t.bank[0][:], ones, gl, start=True, stop=True).then_inc(s["grow"], 1)
                    q, k = qk[:, h, :], qk[:, H + h, :]
                    for src, bank in ((k, 1), (conv[:, 2 * H + h, :], 2)):
                        for b in range(NB):
                            last = tr(t.bank[bank][:, b * P:(b + 1) * P], src[:, b * P:(b + 1) * P], ident)
                        last.then_inc(s["tiles_t"], 1)
                    for left, right, bank in ((k, k, 3), (k, q, 4)):
                        for b in range(NB):
                            w = slice(b * P, (b + 1) * P)
                            last = mm(t.bank[bank][:, w], left[:, w], right[:, w], start=True, stop=True)
                        last.then_inc(s["kk"], 1)
                    pe.wait_ge(s["a"], h + 1)
                    for b in range(NB):
                        last = tr(t.bank[5][:, b * P:(b + 1) * P], am[:, b * P:(b + 1) * P], ident)
                    last.then_inc(s["a_t"], 1)
                    pe.wait_ge(s["prep"], h + 1)
                for level in range(1, LEVELS):
                    done = H * (level - 1)
                    for h in range(H):
                        pe.wait_ge(s["mt"], done + h + 1)
                        if level > 1:
                            pe.wait_ge(s["level"], done - H + h + 1)
                        for b in range(NB):
                            w = slice(b * P, (b + 1) * P)
                            last = mm(t.bank[h][:, w], mt_u[:, h, w], ti[:, h, w], start=True, stop=True)
                        last.then_inc(s["x"], 1)
                    for h in range(H):
                        pe.wait_ge(s["xs"], done + h + 1)
                        if h >= 2:
                            pe.wait_ge(s["level"], done + h - 1)
                        for b in range(NB):
                            w = slice(b * P, (b + 1) * P)
                            if level < LEVELS - 1:
                                mm(t.bank[4 + h % 2][:, w], tt[:, h, w], x_w[:, h, w], start=True, stop=True)
                            last = mm(t.bank[6 + h % 2][:, w], x_w[:, h, w], tt[:, h, w], start=True, stop=True)
                        last.then_inc(s["tx"], 1)
                for h in range(H):
                    pe.wait_ge(s["level"], H * (LEVELS - 2) + h + 1)
                    if h == 0:
                        pe.wait_ge(s["xs"], H * (LEVELS - 1))
                    if h >= 2:
                        pe.wait_ge(s["u"], h - 1)
                        pe.wait_ge(s["w"], h - 1)
                    for b in range(NB):
                        w = slice(b * P, (b + 1) * P)
                        mm(t.bank[h % 2][:, w], tt[:, h, w], vb[:, h, w], start=True, stop=True)
                        last = mm(t.bank[2 + h % 2][:, w], kbg[:, h, w], tt[:, h, w], start=True, stop=True)
                    last.then_inc(s["uw_t"], 1)
                states, vn = (tmp[:, 0, :], tmp[:, 3, :]), tmp[:, 1, :]
                pe.wait_ge(s["zero"], 1)
                pe.wait_ge(s["w"], H)
                for n in range(NCH):
                    b, rows = n // 2, slice(CHUNK * (n % 2), CHUNK * (n % 2) + CHUNK)
                    cols = slice(n * CHUNK, (n + 1) * CHUNK)
                    state = states[n % 2]
                    if n:
                        pe.wait_ge(s["state"], n)
                    for h in range(H):
                        last = mm(t.bank[4][rows, h * P:(h + 1) * P], x_w[:, h, cols], state[:, h * P:(h + 1) * P],
                                  start=True, stop=True)
                    last.then_inc(s["ws"], 1)
                    pe.wait_ge(s["vnew"], n + 1)
                    for h in range(H):
                        last = mm(t.bank[6][:, h * P:(h + 1) * P], kdec[rows, h, b * P:(b + 1) * P],
                                  vn[rows, h * P:(h + 1) * P], start=True, stop=True)
                    last.then_inc(s["ds"], 1)
                    if n:
                        pe.wait_ge(s["o_copy"], n)
                    for h in range(H):
                        o = t.bank[5][:, h * CHUNK:(h + 1) * CHUNK]
                        mm(o, state[:, h * P:(h + 1) * P], qeg[:, h, cols], start=True, stop=False)
                        last = mm(o, vn[rows, h * P:(h + 1) * P], attn[rows, h, cols], start=False, stop=True)
                    last.then_inc(s["out"], 1)
                for h in range(H):
                    pe.wait_ge(s["osq"], h + 1)
                    if h >= 2:
                        pe.wait_ge(s["oroot"], h - 1)
                    mm(t.bank[h % 2][:], ones, sq[:, h, :], start=True, stop=True).then_inc(s["ossq"], 1)


def sparse_stage(t, proj, mix, wq_d, wqi_d, wkv_d, rel_d, buckets_d, strip_d):
    nc = t.nc
    s = {n: t.sem("dsa_" + n) for n in (
        "chain", "weights", "rel", "squared", "sums", "centred", "csq", "csum", "roots", "normed", "kin",
        "latents", "w_t", "w", "up", "up_out", "v_up", "v_out", "strip", "strip_s", "strip_out", "slid", "flip",
        "bias", "bias_m", "dots", "relu", "score", "fenced", "masked", "logits", "centre", "peak", "exp", "prob",
        "prob_t", "turned", "pv", "mixed")}
    v = t.vec
    NUP = H + IH // 2 + H
    QI0, K0 = H, H + IH // 2
    W = T + P
    with ExitStack() as ctx:
        def sb(name, shape):
            return ctx.enter_context(nc.sbuf_tensor("dsa_" + name, shape, F32))

        wq, wqi = sb("wq", [P, 2, H * P]), sb("wqi", [P, 2, IH * IDIM])
        wkv = sb("wkv", [P, 2, 2, H * P])
        rel, buckets, strip = sb("rel", [BUCKETS, H]), sb("buckets", [BUCKETS, W]), sb("strip", [H, W])
        sq, lat = sb("sq", [P, 5, T]), sb("lat", [P, 4, T])
        xc, kin = sb("xc", [P, T]), sb("kin", [P, T])
        root = sb("root", [P, 3, T])
        up = sb("up", [P, NUP, T])
        vt = sb("vt", [P, NB, H * P])
        bias = sb("bias", [P, H, T])
        w_idx = sb("w_idx", [P, NB, IH])
        relu = sb("relu", [P, 2, T])
        score = sb("score", [P, NB, T])
        best = sb("best", [P, 8])
        pr, prt = sb("pr", [P, 2, T]), sb("prt", [P, 2, T])
        lg = root[:, 0:2, :]
        peak, total = sb("peak", [P, 2]), sb("total", [P, 2])
        slid = sq[:, 0:H, :]
        units = [(b, h) for b in range(NB) for h in range(H)]

        with nc.Block() as block:

            @block.sync
            def _(sp):
                sp.dma_start(rel[:], rel_d).then_inc(s["rel"], 16)
                sp.dma_start(buckets[:], buckets_d).then_inc(s["rel"], 16)
                sp.dma_start(wq[:], wq_d).then_inc(s["weights"], 16)
                sp.dma_start(wqi[:], wqi_d).then_inc(s["weights"], 16)
                sp.dma_start(wkv[:], wkv_d).then_inc(s["weights"], 16)
                sp.wait_ge(s["strip_s"], 2)
                sp.dma_start(strip_d, strip[:]).then_inc(s["strip_out"], 16)
                sp.wait_ge(s["strip_out"], 16)
                sp.wait_ge(s["sums"], 3)
                for h in range(H):
                    sp.dma_start(slid[:, h, :], bass.AP(strip_d.tensor, h * W, [[1, P], [1, T]])).then_inc(s["slid"], 16)

            @block.scalar
            def _(act):
                a = nc.scalar.activation
                for i in range(4):
                    a(sq[:, i, :], proj[:, CQ0 + i, PAD:PAD + T], ACT.Square).then_inc(s["squared"], 1)
                act.wait_ge(s["centred"], 1)
                a(sq[:, 4, :], xc[:], ACT.Square).then_inc(s["csq"], 1)
                act.wait_ge(s["sums"], 3)
                eps = v[:, V_EPS:V_EPS + 1]
                a(root[:, 0, :], t.bank[0][:], ACT.Sqrt, scale=1.0 / RANK, bias=eps).then_inc(s["roots"], 1)
                a(root[:, 1, :], t.bank[1][:], ACT.Sqrt, scale=1.0 / RANK, bias=eps).then_inc(s["roots"], 1)
                act.wait_ge(s["csum"], 1)
                a(root[:, 2, :], t.bank[3][:], ACT.Sqrt, scale=1.0 / IDIM, bias=eps).then_inc(s["roots"], 1)
                for j in range(NUP):
                    act.wait_ge(s["up"], j + 1)
                    a(up[:, j, :], t.bank[j % 4][:], ACT.Copy).then_inc(s["up_out"], 1)
                n = 0
                for b in range(1, NB):
                    S = (b + 1) * P
                    for i in range(IH):
                        act.wait_ge(s["dots"], n + 1)
                        if n >= 2:
                            act.wait_ge(s["score"], n - 1)
                        a(relu[:, n % 2, 0:S], t.bank[n % 4][:, 0:S], ACT.Relu).then_inc(s["relu"], 1)
                        n += 1
                for u, (b, h) in enumerate(units):
                    S = (b + 1) * P
                    act.wait_ge(s["peak"], u + 1)
                    if u >= 2:
                        act.wait_ge(s["prob_t"], u - 1)
                    a(pr[:, u % 2, 0:S], lg[:, u % 2, 0:S], ACT.Exp, bias=peak[:, u % 2:u % 2 + 1],
                      accum_out=total[:, u % 2:u % 2 + 1]).then_inc(s["exp"], 1)
                    act.wait_ge(s["prob_t"], u + 1)
                    if u >= 2:
                        act.wait_ge(s["pv"], u - 1)
                    a(prt[:, u % 2, 0:S], t.bank[4 + u % 2][:, 0:S], ACT.Copy).then_inc(s["turned"], 1)
                    act.wait_ge(s["pv"], u + 1)
                    a(mix[:, H + h, b * P:(b + 1) * P], t.bank[6 + u % 2][:, 0:P], ACT.Copy).then_inc(s["mixed"], 1)

            @block.gpsimd
            def _(pool):
                pool.wait_ge(s["bias"], H)
                nc.gpsimd.affine_select(out=bias[:], in_=bias[:], pattern=[[0, H], [-1, T]], base=T - P,
                                        channel_multiplier=1, compare_op=ALU.is_ge, fill=NEG).then_inc(s["bias_m"], 1)
                for b in range(1, NB):
                    pool.wait_ge(s["score"], b * IH)
                    own = score[:, b, b * P:(b + 1) * P]
                    nc.gpsimd.affine_select(out=own, in_=own, pattern=[[-1, P]], base=0, channel_multiplier=1,
                                            compare_op=ALU.is_ge, fill=OUT_OF_REACH).then_inc(s["fenced"], 1)

            @block.vector
            def _(dve):
                chain = [0]

                def link(ins):
                    chain[0] += 1
                    ins.then_inc(s["chain"], 1)
                    dve.wait_ge(s["chain"], chain[0])

                tt_, ts = nc.vector.tensor_tensor, nc.vector.tensor_scalar
                stt = nc.vector.scalar_tensor_tensor
                dve.wait_ge(s["sums"], 1)
                stt(xc[:], t.bank[2][:], -1.0 / IDIM, proj[:, KI0, PAD:PAD + T], ALU.mult, ALU.add).then_inc(s["centred"], 1)
                dve.wait_ge(s["strip"], 1)
                nc.vector.tensor_copy(strip[:, 0:T], t.bank[4][0:H, :]).then_inc(s["strip_s"], 1)
                nc.vector.tensor_copy(strip[:, T:W], t.bank[5][0:H, 0:P]).then_inc(s["strip_s"], 1)
                dve.wait_ge(s["w_t"], 1)
                ts(w_idx[:], blocks(t.bank[7][:])[:, :, 8:8 + IH], IH ** -0.5 * IDIM ** -0.5, None, ALU.mult).then_inc(s["w"], 1)
                for i in range(3):
                    dve.wait_ge(s["roots"], i + 1)
                    link(nc.vector.reciprocal(root[:, i, :], root[:, i, :]))
                dve.wait_ge(s["centred"], 1)
                for i in range(4):
                    g = V_QN + i
                    stt(lat[:, i, :], proj[:, CQ0 + i, PAD:PAD + T], v[:, g:g + 1], root[:, i // 2, :],
                        ALU.mult, ALU.mult).then_inc(s["latents"], 1)
                link(stt(kin[:], xc[:], v[:, V_IG:V_IG + 1], root[:, 2, :], ALU.mult, ALU.mult))
                ts(kin[:], kin[:], v[:, V_IB:V_IB + 1], None, ALU.add).then_inc(s["kin"], 1)
                for b in range(NB):
                    dve.wait_ge(s["v_up"], b + 1)
                    nc.vector.tensor_copy(vt[:, b, :], t.bank[4 + b % 2][:]).then_inc(s["v_out"], 1)
                for h in range(H):
                    dve.wait_ge(s["flip"], h + 1)
                    nc.vector.tensor_copy(bias[:, h, :], t.bank[6 + h % 2][:]).then_inc(s["bias"], 1)
                n = 0
                dve.wait_ge(s["w"], 1)
                for b in range(1, NB):
                    S = (b + 1) * P
                    for i in range(IH):
                        dve.wait_ge(s["relu"], n + 1)
                        if i == 0:
                            ts(score[:, b, 0:S], relu[:, n % 2, 0:S], w_idx[:, b, i:i + 1], None, ALU.mult).then_inc(s["score"], 1)
                        else:
                            dve.wait_ge(s["score"], n)
                            stt(score[:, b, 0:S], relu[:, n % 2, 0:S], w_idx[:, b, i:i + 1], score[:, b, 0:S],
                                ALU.mult, ALU.add).then_inc(s["score"], 1)
                        n += 1
                for b in range(1, NB):
                    S = (b + 1) * P
                    dve.wait_ge(s["fenced"], b)
                    sc = score[:, b, 0:S]
                    for _ in range(TOPK // 8):
                        link(nc.vector.max(best[:], sc))
                        link(nc.vector.match_replace(sc, best[:], sc, TAKEN))
                    ts(sc, sc, TAKEN, NEG, ALU.not_equal, ALU.mult).then_inc(s["masked"], 1)
                dve.wait_ge(s["masked"], NB - 1)
                dve.wait_ge(s["bias_m"], 1)

                def logits(u):
                    b, h = units[u]
                    S, o = (b + 1) * P, (NB - 1 - b) * P
                    l = lg[:, u % 2, 0:S]
                    dve.wait_ge(s["logits"], u + 1)
                    if u >= 2:
                        dve.wait_ge(s["exp"], u - 1)
                    link(stt(l, t.bank[u % 2][:, 0:S], P ** -0.5, bias[:, h, o:o + S], ALU.mult, ALU.add))
                    if b:
                        link(tt_(l, l, score[:, b, 0:S], ALU.add))
                    nc.vector.tensor_reduce(peak[:, u % 2:u % 2 + 1], l, AX.X, ALU.max, negate=True).then_inc(s["peak"], 1)

                def probabilities(u):
                    S = (units[u][0] + 1) * P
                    r = total[:, u % 2:u % 2 + 1]
                    dve.wait_ge(s["exp"], u + 1)
                    link(nc.vector.reciprocal(r, r))
                    ts(pr[:, u % 2, 0:S], pr[:, u % 2, 0:S], r, None, ALU.mult).then_inc(s["prob"], 1)

                logits(0)
                for u in range(len(units)):
                    if u + 1 < len(units):
                        logits(u + 1)
                    probabilities(u)

            @block.tensor
            def _(pe):
                mm, tr = nc.tensor.matmul, nc.tensor.transpose
                ident, ones = t.c(C_ID), t.c(C_ONES)
                mm(t.bank[2][:], t.c(C_SAME), proj[:, KI0, PAD:PAD + T], start=True, stop=True).then_inc(s["sums"], 1)
                pe.wait_ge(s["rel"], 32)
                mm(t.bank[4][0:H, :], rel[:], buckets[:, 0:T], start=True, stop=True)
                mm(t.bank[5][0:H, 0:P], rel[:], buckets[:, T:W], start=True, stop=True).then_inc(s["strip"], 1)
                for b in range(NB):
                    last = tr(t.bank[7][:, b * P:(b + 1) * P], proj[:, AB0, PAD + b * P:PAD + (b + 1) * P], ident)
                last.then_inc(s["w_t"], 1)
                for i in range(2):
                    pe.wait_ge(s["squared"], 2 * i + 2)
                    mm(t.bank[i][:], ones, sq[:, 2 * i, :], start=True, stop=False)
                    mm(t.bank[i][:], ones, sq[:, 2 * i + 1, :], start=False, stop=True).then_inc(s["sums"], 1)
                pe.wait_ge(s["csq"], 1)
                mm(t.bank[3][:], t.c(C_SAME), sq[:, 4, :], start=True, stop=True).then_inc(s["csum"], 1)
                pe.wait_ge(s["weights"], 48)
                pe.wait_ge(s["latents"], 4)
                pe.wait_ge(s["roots"], 3)
                for j in range(NUP):
                    if j >= 4:
                        pe.wait_ge(s["up_out"], j - 3)
                    for c in range(2):
                        if j < QI0:
                            left, right = wq[:, c, j * P:(j + 1) * P], lat[:, c, :]
                        elif j < K0:
                            left, right = wqi[:, c, (j - QI0) * P:(j - QI0 + 1) * P], lat[:, c, :]
                        else:
                            left, right = wkv[:, c, 0, (j - K0) * P:(j - K0 + 1) * P], lat[:, 2 + c, :]
                        last = mm(t.bank[j % 4][:], left, right, start=c == 0, stop=c == 1)
                    last.then_inc(s["up"], 1)
                pe.wait_ge(s["strip_s"], 2)
                for b in range(NB):
                    if b >= 2:
                        pe.wait_ge(s["v_out"], b - 1)
                    for c in range(2):
                        last = mm(t.bank[4 + b % 2][:], lat[:, 2 + c, b * P:(b + 1) * P], wkv[:, c, 1, :],
                                  start=c == 0, stop=c == 1)
                    last.then_inc(s["v_up"], 1)
                pe.wait_ge(s["w"], 1)
                for h in range(H):
                    pe.wait_ge(s["slid"], 16 * H)
                    if h >= 2:
                        pe.wait_ge(s["bias"], h - 1)
                    mm(t.bank[6 + h % 2][:], t.c(C_ANTI), slid[:, h, :], start=True, stop=True).then_inc(s["flip"], 1)
                pe.wait_ge(s["up_out"], NUP)
                pe.wait_ge(s["kin"], 1)
                n = 0
                for b in range(1, NB):
                    S = (b + 1) * P
                    for i in range(IH):
                        if n >= 4:
                            pe.wait_ge(s["relu"], n - 3)
                        rows = slice(IDIM * (i % 2), IDIM * (i % 2) + IDIM)
                        mm(t.bank[n % 4][:, 0:S], up[rows, QI0 + i // 2, b * P:(b + 1) * P], kin[rows, 0:S],
                           start=True, stop=True).then_inc(s["dots"], 1)
                        n += 1
                pe.wait_ge(s["relu"], n)
                pe.wait_ge(s["bias"], H)
                pe.wait_ge(s["v_out"], NB)

                def logits(u):
                    b, h = units[u]
                    if u >= 2:
                        pe.wait_ge(s["peak"], u - 1)
                    mm(t.bank[u % 2][:, 0:(b + 1) * P], up[:, h, b * P:(b + 1) * P], up[:, K0 + h, 0:(b + 1) * P],
                       start=True, stop=True).then_inc(s["logits"], 1)

                logits(0)
                for u, (b, h) in enumerate(units):
                    if u + 1 < len(units):
                        logits(u + 1)
                    pe.wait_ge(s["prob"], u + 1)
                    if u >= 2:
                        pe.wait_ge(s["turned"], u - 1)
                    for k in range(b + 1):
                        last = tr(t.bank[4 + u % 2][:, k * P:(k + 1) * P], pr[:, u % 2, k * P:(k + 1) * P], ident)
                    last.then_inc(s["prob_t"], 1)
                    pe.wait_ge(s["turned"], u + 1)
                    if u >= 2:
                        pe.wait_ge(s["mixed"], u - 1)
                    for k in range(b + 1):
                        last = mm(t.bank[6 + u % 2][:, 0:P], vt[:, k, h * P:(h + 1) * P], prt[:, u % 2, k * P:(k + 1) * P],
                                  start=k == 0, stop=k == b)
                    last.then_inc(s["pv"], 1)


def route_stage(t, qy, hi, lo, u_d, keys_d, gates_d, active_d):
    nc = t.nc
    N, BODY = PK, 16
    TOK = 8
    ld_u = [t.sem(f"rt_u_loaded{i}") for i in range(2)]
    kept_a = [t.sem(f"rt_active_stored{i}") for i in range(2)]
    sent = [t.sem(f"rt_chunk_sent{i}") for i in range(2)]
    u_high, u_low, first, active = (t.sem("rt_" + k) for k in ("u_high", "u_low", "first", "active"))
    s = {n: t.sem("rt_" + n) for n in (
        "chain", "keys", "picked", "scores", "taken", "tops", "exps", "chosen", "slots_t", "slots", "gate_low",
        "hot", "hot2", "placed", "copied")}
    with ExitStack() as ctx:
        def sb(name, shape, dt=F32):
            return ctx.enter_context(nc.sbuf_tensor("rt_" + name, shape, dt))

        u_raw, act_s = sb("u_raw", [P, 2, D]), sb("act", [P, 2, T])
        u_hi, u_lo = sb("u_hi", [P, 2, D], F32R), sb("u_lo", [P, 2, D], F32R)
        early = sb("early", [P, PK * CH])
        size = 2 * PH * P
        keys, qb = (early[:, k * size:(k + 1) * size].rearrange("p (a b) -> p a b", b=P) for k in range(2))
        hit = early[:, 2 * size:3 * size].rearrange("p (h a b) -> p h a b", h=PH, a=PTOP)
        val = sb("val", [P, 2, PTOP])
        num = sb("num", [P, 2, PH, PTOP], U32)
        pos, top = sb("pos", [P, PH, PTOP], U32), sb("top", [P, PH, PTOP])
        work = sb("work", [P, 2, PK])
        cand, cwork = sb("cand", [P, PTOP * PTOP]), sb("cwork", [P, PTOP * PTOP])
        part = sb("part", [P, 2, PH, PTOP], U32)
        part_f, num_f = sb("part_f", [P, 2, PH, PTOP]), sb("num_f", [P, 2, PH, PTOP])
        peak, total = sb("peak", [P, PH]), sb("total", [P, PH])
        out = sb("out", [P, 3, PH * PTOP])
        slot1, slot2, gate = sb("slot1", [P, T]), sb("slot2", [P, T]), sb("gate", [P, T])
        gate_hi, gate_lo = sb("gate_hi", [P, T], F32R), sb("gate_lo", [P, T])
        hot2 = sb("hot2", [P, TOK, P])
        hot1 = sb("hot1", [P, 2, TOK, P], F32R)
        hot2h, hot2l = sb("hot2h", [P, 2, TOK, P], F32R), sb("hot2l", [P, 2, TOK, P], F32R)
        table = [ap.rearrange("p (e n) -> p e n", e=PK) for ap in (early[:], qy[:].rearrange("p a b -> p (a b)"))]

        def run(eng, slot, tail=None):
            for phase in range(2):
                for j in range(BODY):
                    slot(phase, 0, j, True)
                with eng.Fori(1, N // BODY // 2) as i:
                    for j in range(BODY):
                        slot(phase, i, j, False)
            if tail:
                tail()

        def number(phase, i, j):
            return N // 2 * phase + BODY * i + j

        with nc.Block() as block:

            @block.sync
            def _(sp):
                sp.dma_start(keys, keys_d).then_inc(s["keys"], 16)

                def load(e, par, free):
                    if free:
                        sp.wait_ge(u_low, e - 1)
                    sp.dma_start(u_raw[:, par, :], u_d[e]).then_inc(ld_u[par], 16)

                def store(e, par):
                    sp.wait_ge(active, e + 1)
                    sp.dma_start(active_d[e], act_s[:, par, :]).then_inc(kept_a[par], 16)

                load(0, 0, False)
                load(1, 1, False)
                with sp.Fori(1, N // 2) as i:
                    for par in range(2):
                        load(2 * i + par, par, True)
                        store(2 * i + par - 2, par)
                store(N - 2, 0)
                store(N - 1, 1)
                for par in range(2):
                    sp.wait_ge(kept_a[par], 16 * (N // 2))

            @block.scalar
            def _(act):
                a = nc.scalar.activation

                def gelu(e, par, uses):
                    act.wait_ge(first, e + 1)
                    if uses is not None:
                        act.wait_ge(kept_a[par], 16 * uses)
                    a(act_s[:, par, :], t.bank[par][:], ACT.Gelu).then_inc(active, 1)

                def copy_out(i, j, c_uses):
                    par, local = j // 8, j % 8
                    if local == 0 and c_uses is not None:
                        act.wait_ge(sent[par], 16 * c_uses)
                    for g in range(2):
                        act.wait_ge(s["placed"], 2 * (BODY * i + j) + g + 1)
                        a(table[par][:, :, local * TOK + 4 * g:local * TOK + 4 * g + 4],
                          t.bank[2 + 2 * (j % 2) + g][:].rearrange("p (k e) -> p e k", k=4), ACT.Copy).then_inc(s["copied"], 1)
                    if local == 7:
                        act.wait_ge(s["copied"], 2 * (BODY * i + j) + 2)
                        act.dma_start(gates_d[:, bass.ds(2 * i + par, 1), :, :],
                                      table[par]).then_inc(sent[par], 16)

                def slot(phase, i, j, head):
                    e = number(phase, i, j)
                    if phase == 0 and j == 0:
                        if not head:
                            act.wait_ge(s["scores"], PH * i)
                        a(qb, qy[:, :, bass.ds(i * P, P)], ACT.Copy).then_inc(s["picked"], 1)
                    act.wait_ge(ld_u[j % 2], 16 * (N // 4 * phase + BODY // 2 * i + j // 2 + 1))
                    fresh = head and phase == 0 and j < 2
                    if not fresh:
                        act.wait_ge(first, e - 1)
                    a(u_hi[:, j % 2, :], u_raw[:, j % 2, :], ACT.Copy).then_inc(u_high, 1)
                    if not (head and phase == 0 and j == 0):
                        old = not (head and phase == 0 and j < 3)
                        gelu(e - 1, (j - 1) % 2, N // 4 * phase + BODY // 2 * i + (j - 1) // 2 if old else None)
                    if phase == 0 and j == BODY - 1:
                        act.wait_ge(s["slots_t"], i + 1)
                        turned = t.bank[6]
                        cols = bass.ds(i * P, P)
                        a(slot1[:, cols], turned[:, 0:P], ACT.Copy)
                        a(slot2[:, cols], turned[:, P:2 * P], ACT.Copy)
                        a(gate[:, cols], turned[:, 2 * P:3 * P], ACT.Copy)
                        a(gate_hi[:, cols], turned[:, 2 * P:3 * P], ACT.Copy).then_inc(s["slots"], 1)
                    if phase == 0 and j == BODY - 4:
                        act.wait_ge(s["tops"], i + 1)
                        a(top[:], top[:], ACT.Exp).then_inc(s["exps"], 1)
                    if phase == 1:
                        if j:
                            copy_out(i, j - 1, i if not head else None)
                        elif not head:
                            copy_out(i - 1, BODY - 1, None)

                def tail():
                    gelu(N - 1, 1, N // 2 - 1)
                    copy_out(3, BODY - 1, None)
                    for par in range(2):
                        act.wait_ge(sent[par], 16 * 4)
                run(act, slot, tail)

            @block.gpsimd
            def _(pool):
                def low(e, par):
                    pool.wait_ge(u_high, e + 1)
                    nc.gpsimd.tensor_tensor(u_lo[:, par, :], u_raw[:, par, :], u_hi[:, par, :].bitcast(F32),
                                            ALU.subtract).then_inc(u_low, 1)
                with pool.Fori(0, N // 2) as i:
                    for par in range(2):
                        low(2 * i + par, par)

            @block.vector
            def _(dve):
                d = nc.vector

                def chosen_block(i, head):
                    links = [0]
                    per = PH * 8 + 9

                    def link(ins):
                        links[0] += 1
                        ins.then_inc(s["chain"], 1)
                        dve.wait_ge(s["chain"], per * i + links[0])

                    for h in range(PH):
                        u = PH * i + h
                        dve.wait_ge(s["scores"], u + 1)
                        sc = [t.bank[2 + h % 4][:, side * PK:(side + 1) * PK] for side in range(2)]
                        d.max(val[:, 0, 0:8], sc[0])
                        link(d.max(val[:, 1, 0:8], sc[1]))
                        for side in range(2):
                            d.max_index(num[:, side, h, 0:8], val[:, side, 0:8], sc[side])
                            ins = d.match_replace(work[:, side, :], val[:, side, 0:8], sc[side], TAKEN)
                        ins.then_inc(s["taken"], 1)
                        dve.wait_ge(s["taken"], u + 1)
                        d.max(val[:, 0, 8:16], work[:, 0, :])
                        link(d.max(val[:, 1, 8:16], work[:, 1, :]))
                        for side in range(2):
                            d.max_index(num[:, side, h, 8:16], val[:, side, 8:16], work[:, side, :])
                        link(d.tensor_tensor(cand[:].rearrange("p (a b) -> p a b", a=PTOP),
                                             val[:, 0, :].unsqueeze(2).to_broadcast([P, PTOP, PTOP]),
                                             val[:, 1, :].unsqueeze(1).to_broadcast([P, PTOP, PTOP]), ALU.add))
                        link(d.max(top[:, h, 0:8], cand[:]))
                        d.max_index(pos[:, h, 0:8], top[:, h, 0:8], cand[:])
                        link(d.match_replace(cwork[:], top[:, h, 0:8], cand[:], TAKEN))
                        link(d.max(top[:, h, 8:16], cwork[:]))
                        link(d.max_index(pos[:, h, 8:16], top[:, h, 8:16], cwork[:]))
                        link(d.tensor_copy(peak[:, h:h + 1], top[:, h, 0:1]))
                    d.tensor_tensor(top[:], top[:], peak[:].unsqueeze(2).to_broadcast([P, PH, PTOP]),
                                    ALU.subtract).then_inc(s["tops"], 1)
                    d.tensor_scalar(part[:, 0], pos[:], 4, None, ALU.logical_shift_right)
                    link(d.tensor_scalar(part[:, 1], pos[:], PTOP - 1, None, ALU.bitwise_and))
                    d.tensor_copy(part_f[:], part[:])
                    link(d.tensor_copy(num_f[:], num[:]))
                    if not head:
                        dve.wait_ge(s["slots_t"], i)
                    iota = t.c(C_IOTA)[:, 0:PTOP].unsqueeze(1).unsqueeze(1).to_broadcast([P, PH, PTOP, PTOP])
                    for side in range(2):
                        link(d.tensor_tensor(hit, part_f[:, side].unsqueeze(3).to_broadcast([P, PH, PTOP, PTOP]),
                                             iota, ALU.is_equal))
                        link(d.tensor_tensor(hit, hit, num_f[:, side].unsqueeze(2).to_broadcast([P, PH, PTOP, PTOP]),
                                             ALU.mult))
                        ins = d.tensor_reduce(out[:, side, :].rearrange("p (h k) -> p h k", h=PH), hit, AX.X, ALU.add)
                        if side == 0:
                            link(ins)
                    dve.wait_ge(s["exps"], i + 1)
                    link(d.tensor_reduce(total[:], top[:], AX.X, ALU.add))
                    link(d.reciprocal(total[:], total[:]))
                    d.tensor_tensor(out[:, 2, :].rearrange("p (h k) -> p h k", h=PH), top[:],
                                    total[:].unsqueeze(2).to_broadcast([P, PH, PTOP]), ALU.mult).then_inc(s["chosen"], 1)
                    assert links[0] == per, links

                for i in range(NB):
                    chosen_block(i, i == 0)
                dve.wait_ge(s["slots"], NB)
                d.tensor_tensor(gate_lo[:], gate[:], gate_hi[:].bitcast(F32), ALU.subtract).then_inc(s["gate_low"], 1)
                dve.wait_ge(s["gate_low"], 1)
                iota = t.c(C_IOTA)

                def hots(i, j, head):
                    cols = bass.ds((2 * i + j) * TOK, TOK)

                    def wide(ap):
                        return ap[:, cols].unsqueeze(2).to_broadcast([P, TOK, P])
                    keys_row = iota.unsqueeze(1).to_broadcast([P, TOK, P])
                    if not head:
                        dve.wait_ge(s["placed"], 4 * i + 2 * j - 2)
                    if not (head and j == 0):
                        dve.wait_ge(s["hot"], 2 * i + j)
                    d.tensor_tensor(hot2[:], keys_row, wide(slot2), ALU.is_equal).then_inc(s["hot2"], 1)
                    d.tensor_tensor(hot1[:, j], keys_row, wide(slot1), ALU.is_equal)
                    dve.wait_ge(s["hot2"], 2 * i + j + 1)
                    d.tensor_tensor(hot2h[:, j], hot2[:], wide(gate_hi[:].bitcast(F32)), ALU.mult)
                    d.tensor_tensor(hot2l[:, j], hot2[:], wide(gate_lo), ALU.mult).then_inc(s["hot"], 1)

                hots(0, 0, True)
                hots(0, 1, True)
                with dve.Fori(1, T // TOK // 2) as i:
                    hots(i, 0, False)
                    hots(i, 1, False)

            @block.tensor
            def _(pe):
                mm = nc.tensor.matmul
                pe.wait_ge(s["keys"], 16)

                def slot(phase, i, j, head):
                    e = number(phase, i, j)
                    if phase == 0 and j < PH:
                        h = j
                        if j == 0:
                            pe.wait_ge(s["picked"], i + 1)
                        if not (head and h < 4):
                            pe.wait_ge(s["taken"], PH * i + h - 3)
                        for side in range(2):
                            last = mm(t.bank[2 + h % 4][:, side * PK:(side + 1) * PK], qb[:, 2 * h + side, :],
                                      keys[:, 2 * h + side, :], start=True, stop=True)
                        last.then_inc(s["scores"], 1)
                    if phase == 0 and j == BODY - 1:
                        pe.wait_ge(s["chosen"], i + 1)
                        if not head:
                            pe.wait_ge(s["slots"], i)
                        for k in range(3):
                            last = nc.tensor.transpose(t.bank[6][:, k * P:(k + 1) * P], out[:, k, :], t.c(C_ID))
                        last.then_inc(s["slots_t"], 1)
                    pe.wait_ge(u_low, e + 1)
                    if not (head and phase == 0 and j < 2):
                        pe.wait_ge(active, e - 1)
                    bank = t.bank[j % 2][:]
                    for c in range(DC):
                        cols = slice(c * P, (c + 1) * P)
                        mm(bank, u_hi[:, j % 2, cols], hi[:, c, :], start=c == 0, stop=False)
                        mm(bank, u_hi[:, j % 2, cols], lo[:, c, :], start=False, stop=False)
                        last = mm(bank, u_lo[:, j % 2, cols], hi[:, c, :], start=False, stop=c == DC - 1)
                    last.then_inc(first, 1)
                    if phase == 1:
                        step = BODY * i + j
                        pe.wait_ge(s["hot"], step + 1)
                        for g in range(2):
                            if not (head and j < 2):
                                pe.wait_ge(s["copied"], 2 * step + g - 3)
                            for k in range(4):
                                o, tok = t.bank[2 + 2 * (j % 2) + g][:, k * P:(k + 1) * P], 4 * g + k
                                mm(o, hot1[:, j % 2, tok, :], hot2h[:, j % 2, tok, :], start=True, stop=False)
                                last = mm(o, hot1[:, j % 2, tok, :], hot2l[:, j % 2, tok, :], start=False, stop=True)
                            last.then_inc(s["placed"], 1)
                run(pe, slot)


def value_stage(t, x, v_d, gates_d, active_d):
    nc = t.nc
    N = PK

    ld_v, ld_w, ld_g = ([t.sem(f"va_{k}_loaded{i}") for i in range(2)] for k in ("v", "w", "gates"))
    v_high, v_low, gated, w_high, w_low, second, added = (
        t.sem("va_" + k) for k in ("v_high", "v_low", "gated", "w_high", "w_low", "second", "added"))
    with ExitStack() as ctx:
        def sb(name, shape, dt=F32):
            return ctx.enter_context(nc.sbuf_tensor("va_" + name, shape, dt))

        v_raw = sb("v_raw", [P, 2, D])
        v_hi, v_lo = sb("v_hi", [P, 2, D], F32R), sb("v_lo", [P, 2, D], F32R)
        gate = sb("gate", [P, 2, T // CH, 2, CH])
        act_s, w = sb("act", [P, 2, T]), sb("w", [P, 2, T])
        w_hi, w_lo = sb("w_hi", [P, 2, T], F32R), sb("w_lo", [P, 2, T], F32R)

        def run(eng, slot, n=N // 2):
            slot(0, 0, True)
            slot(0, 1, True)
            with eng.Fori(1, n // 2) as i:
                slot(i, 0, False)
                slot(i, 1, False)

        with nc.Block() as block:

            @block.sync
            def _(sp):
                def pair(i, q, head):
                    u = 2 * i + q
                    if not head:
                        sp.wait_ge(gated, 2 * u - 2)
                    sp.dma_start(gate[:, q], gates_d[:, :, bass.ds(2 * u, 2), :]).then_inc(ld_g[q], 16)
                    for j in range(2):
                        e = 2 * u + j
                        if not (head and q == 0):
                            sp.wait_ge(v_low, e - 1)
                        sp.dma_start(v_raw[:, j, :], v_d[:, e, :]).then_inc(ld_v[j], 16)
                        if not (head and q == 0):
                            sp.wait_ge(gated, e - 1)
                        sp.dma_start(act_s[:, j, :], active_d[e]).then_inc(ld_w[j], 16)
                run(sp, pair)

            @block.scalar
            def _(act):
                def pair(i, q, head):
                    u = 2 * i + q
                    for j in range(2):
                        e = 2 * u + j
                        act.wait_ge(ld_v[j], 16 * (u + 1))
                        if not (head and q == 0):
                            act.wait_ge(second, e - 1)
                        nc.scalar.activation(v_hi[:, j, :], v_raw[:, j, :], ACT.Copy).then_inc(v_high, 1)
                        act.wait_ge(gated, e + 1)
                        nc.scalar.activation(w_hi[:, j, :], w[:, j, :], ACT.Copy).then_inc(w_high, 1)
                run(act, pair)

            @block.vector
            def _(dve):
                def minus(out, a, high, done):
                    nc.vector.tensor_tensor(out, a, high.bitcast(F32), ALU.subtract).then_inc(done, 1)

                def pair(i, q, head):
                    u = 2 * i + q
                    dve.wait_ge(ld_g[q], 16 * (i + 1))
                    for j in range(2):
                        e = 2 * u + j
                        dve.wait_ge(ld_w[j], 16 * (u + 1))
                        chunks = [ap[:, j, :].rearrange("p (c n) -> p c n", n=CH) for ap in (w, act_s)]
                        nc.vector.tensor_tensor(chunks[0], chunks[1], gate[:, q, :, j, :], ALU.mult).then_inc(gated, 1)
                        dve.wait_ge(v_high, e + 1)
                        minus(v_lo[:, j, :], v_raw[:, j, :], v_hi[:, j, :], v_low)
                        dve.wait_ge(w_high, e + 1)
                        minus(w_lo[:, j, :], w[:, j, :], w_hi[:, j, :], w_low)
                run(dve, pair)
                dve.wait_ge(second, N)
                for d in range(DC):
                    nc.vector.tensor_tensor(x[:, d, :], x[:, d, :], t.bank[d][:], ALU.add).then_inc(added, 1)

            @block.tensor
            def _(pe):
                mm = nc.tensor.matmul

                def slot(i, j, start=False, stop=False):
                    e = 2 * i + j
                    pe.wait_ge(v_low, e + 1)
                    pe.wait_ge(w_low, e + 1)
                    for d in range(DC):
                        bank, cols = t.bank[d][:], slice(d * P, (d + 1) * P)
                        mm(bank, v_hi[:, j, cols], w_hi[:, j, :], start=start, stop=False)
                        mm(bank, v_hi[:, j, cols], w_lo[:, j, :], start=False, stop=False)
                        last = mm(bank, v_lo[:, j, cols], w_hi[:, j, :], start=False, stop=stop)
                    last.then_inc(second, 1)

                slot(0, 0, start=True)
                slot(0, 1)
                with pe.Fori(1, N // 2 - 1) as i:
                    slot(i, 0)
                    slot(i, 1)
                slot(N // 2 - 1, 0)
                slot(N // 2 - 1, 1, stop=True)


def store_stage(t, y, out_d):
    nc = t.nc
    stored = t.sem("stored")
    with nc.Block() as block:

        @block.sync
        def _(sp):
            sp.dma_start(out_d, y[:]).then_inc(stored, 16)
            sp.wait_ge(stored, 16)


def build(nc, a):
    with ExitStack() as outer:
        t = Tables(nc, outer)
        x = outer.enter_context(nc.sbuf_tensor("x_stream", [P, DC, T], F32))
        load_stage(t, a["x"], a["constants"], a["vectors"], x)
        with ExitStack() as mixers:
            mix = mixers.enter_context(nc.sbuf_tensor("mix", [P, 2 * H, T], F32))
            with ExitStack() as inner:
                proj = inner.enter_context(nc.sbuf_tensor("proj", [P, NPROJ, PAD + T + 1], F32))
                zeroed = t.sem("pad_zeroed")
                with nc.Block() as block:

                    @block.vector
                    def _(dve):
                        nc.vector.memset(proj[:, :, 0:PAD], 0.0).then_inc(zeroed, 1)
                with ExitStack() as split:
                    hi = split.enter_context(nc.sbuf_tensor("h1_hi", [P, DC, T], F32R))
                    lo = split.enter_context(nc.sbuf_tensor("h1_lo", [P, DC, T], F32R))
                    norm_stage(t, "ln1", x, V_LN1, hi, lo)
                    project_stage(t, "in", a["w_in"], NPROJ, hi, lo, lambda i: proj[:, i, PAD:PAD + T])
                delta_stage(t, proj, mix)
                sparse_stage(t, proj, mix, a["w_q_up"], a["w_qidx_up"], a["w_kv_up"], a["rel_bias"],
                             a["buckets"], a["strip"])
            with ExitStack() as split:
                hi = split.enter_context(nc.sbuf_tensor("mix_hi", [P, DC, T], F32R))
                lo = split.enter_context(nc.sbuf_tensor("mix_lo", [P, DC, T], F32R))
                split_stage(t, "mix", mix, hi, lo)
                project_stage(t, "out", a["w_out"], DC, hi, lo, lambda i: x[:, i, :], add=lambda i: x[:, i, :])
        t.free_semaphores()
        with ExitStack() as peer:
            hi = peer.enter_context(nc.sbuf_tensor("h2_hi", [P, DC, T], F32R))
            lo = peer.enter_context(nc.sbuf_tensor("h2_lo", [P, DC, T], F32R))
            norm_stage(t, "ln2", x, V_LN2, hi, lo)
            with ExitStack() as route:
                qy = route.enter_context(nc.sbuf_tensor("qy", [P, 2 * PH, T], F32))
                project_stage(t, "query", a["w_query"], 2 * PH, hi, lo, lambda i: qy[:, i, :])
                route_stage(t, qy, hi, lo, a["u"], a["keys"], a["gates"], a["active"])
        value_stage(t, x, a["v"], a["gates"], a["active"])
        y = outer.enter_context(nc.sbuf_tensor("y", [P, DC, T], F32))
        norm_stage(t, "final", x, V_FIN, out=y)
        store_stage(t, y, a["out"])


def split_stage(t, tag, src, hi, lo):
    nc = t.nc
    high, low = t.sem(tag + "_split_high"), t.sem(tag + "_split_low")
    with nc.Block() as block:

        @block.scalar
        def _(act):
            for c in range(DC):
                nc.scalar.activation(hi[:, c, :], src[:, c, :], ACT.Copy).then_inc(high, 1)

        @block.vector
        def _(dve):
            for c in range(DC):
                dve.wait_ge(high, c + 1)
                nc.vector.tensor_tensor(lo[:, c, :], src[:, c, :], hi[:, c, :].bitcast(F32),
                                        ALU.subtract).then_inc(low, 1)


def tiles(w, n):
    return np.ascontiguousarray(w.reshape(DC, P, n, P).transpose(2, 1, 0, 3)).reshape(n, P, D)


def layout(inputs):
    f = {k: np.asarray(v) for k, v in inputs.items()}
    w_in = f["w_in"][0]
    ab = 4 * H * P
    rest = ab + 2 * H
    idx = rest + 2 * RANK
    cols = [w_in[:, 0:ab], w_in[:, rest:idx], w_in[:, idx:idx + IDIM], w_in[:, idx:idx + IDIM],
            w_in[:, ab:rest], w_in[:, idx + IDIM:], np.zeros((D, P - 2 * H - IH), np.float32)]
    vec = np.zeros((P, V_N), np.float32)
    vec[:, V_LN1:V_LN1 + DC] = f["ln1_g"][0].reshape(DC, P).T
    vec[:, V_LN2:V_LN2 + DC] = f["ln2_g"][0].reshape(DC, P).T
    vec[:, V_FIN:V_FIN + DC] = f["final_g"].reshape(DC, P).T
    vec[:, V_CONV:V_CONV + 3 * H * CONV] = f["conv_w"][0].reshape(CONV, 3 * H, P).transpose(2, 1, 0).reshape(P, -1)
    vec[:, V_GDN] = f["gdn_norm_g"][0]
    vec[:, V_QN:V_QN + 2] = f["q_norm_g"][0].reshape(2, P).T
    vec[:, V_KVN:V_KVN + 2] = f["kv_norm_g"][0].reshape(2, P).T
    vec[:, V_IG] = np.concatenate([f["idx_ln_g"][0]] * 2)
    vec[:, V_IB] = np.concatenate([f["idx_ln_b"][0]] * 2)
    vec[:, V_EPS] = EPS
    vec[:, V_ALOG:V_ALOG + H] = f["a_log"][0]
    vec[:, V_DTB:V_DTB + H] = f["dt_bias"][0]
    keys = np.stack([f["peer_sub_keys_1"][0], f["peer_sub_keys_2"][0]], axis=1)
    return {
        "x": np.ascontiguousarray(f["x"][0].T.reshape(DC, P, T).transpose(1, 0, 2)),
        "constants": constants(), "vectors": vec, "buckets": bucket_rows(),
        "w_in": tiles(np.concatenate(cols, axis=1), NPROJ),
        "w_q_up": np.ascontiguousarray(f["w_q_up"][0].reshape(2, P, -1).transpose(1, 0, 2)),
        "w_qidx_up": np.ascontiguousarray(f["w_qidx_up"][0].reshape(2, P, -1).transpose(1, 0, 2)),
        "w_kv_up": np.ascontiguousarray(f["w_kv_up"][0].reshape(2, P, H, 2, P).transpose(1, 0, 3, 2, 4)).reshape(P, 2, 2, H * P),
        "rel_bias": f["rel_bias"],
        "w_out": tiles(f["w_out"][0], DC),
        "w_query": tiles(f["peer_w_query"][0], 2 * PH),
        "keys": np.ascontiguousarray(keys.reshape(2 * PH, PK, P).transpose(2, 0, 1)),
        "u": np.ascontiguousarray(f["peer_u"][0].reshape(PK, PK, DC, P).transpose(1, 3, 2, 0)).reshape(PK, P, D),
        "v": f["peer_v"][0].reshape(PK, PK, D),
    }


def kernel(**inputs):
    import concourse.bacc as bacc
    from concourse.bass_utils import run_bass_kernel_spmd

    nc = bacc.Bacc("TRN2", target_bir_lowering=False, num_devices=1)
    arrays = layout(inputs)
    a = {k: nc.dram_tensor(k + "_dram", v.shape, F32, kind="ExternalInput").ap() for k, v in arrays.items()}
    a["out"] = nc.dram_tensor("out_dram", (P, DC, T), F32, kind="ExternalOutput").ap()
    a["strip"] = nc.dram_tensor("strip_scratch", (H, T + P), F32).ap()
    a["active"] = nc.dram_tensor("active_scratch", (PK, P, T), F32).ap()
    a["gates"] = nc.dram_tensor("gates_scratch", (P, T // CH, PK, CH), F32).ap()
    build(nc, a)
    r = run_bass_kernel_spmd(nc, [{k + "_dram": v for k, v in arrays.items()}], core_ids=[0])
    out = r.results[0]["out_dram"]
    return np.ascontiguousarray(out.transpose(1, 0, 2).reshape(D, T).T).reshape(1, T, D)
```

```python
from contextlib import ExitStack
import math

import numpy as np
import concourse.bass as bass
from concourse import mybir

F32 = mybir.dt.float32
F32R = mybir.dt.float32r
U32 = mybir.dt.uint32
ACT = mybir.ActivationFunctionType
ALU = mybir.AluOpType
AX = mybir.AxisListType

P = 128
T = 512
NB = T // P
D = 1024
DC = D // P
H = 4
CONV = 4
CHUNK = 64
NCH = T // CHUNK
RANK = 256
IH, IDIM = 16, 64
TOPK = 128
BUCKETS = 32
PH, PK, PTOP = 8, 128, 16
CH = 64
EPS = 1e-6
PAD = CONV - 1

QKV_T = 3 * H
Z0, CQ0, CKV0, KI0, AB0 = 12, 16, 18, 20, 21
NPROJ = 22
NEG = -1e30
TAKEN = -3.0e38
OUT_OF_REACH = -2.0e38

C_ID, C_ONES, C_CUM, C_STRICT, C_SAME, C_HALF0, C_ANTI, C_IOTA, C_M0, C_MT = 0, 1, 2, 3, 4, 5, 7, 8, 9, 10
LEVELS = 6
C_N = C_MT + LEVELS
V_LN1, V_LN2, V_FIN, V_CONV, V_GDN, V_QN, V_KVN, V_IG, V_IB, V_EPS, V_ALOG, V_DTB, V_QK, V_N = (
    0, 8, 16, 24, 72, 73, 75, 77, 78, 79, 80, 84, 88, 96)


def constants():
    r, c = np.arange(P)[:, None], np.arange(P)[None, :]
    same = r // CHUNK == c // CHUNK
    t = np.zeros((P, C_N, P), np.float32)
    t[:, C_ID] = r == c
    t[:, C_ONES] = 1
    t[:, C_CUM] = same & (r <= c)
    t[:, C_STRICT] = same & (c < r)
    t[:, C_SAME] = same
    t[:, C_HALF0] = (r < CHUNK) & (c >= 0)
    t[:, C_HALF0 + 1] = (r >= CHUNK) & (c >= 0)
    t[:, C_ANTI] = r + c == P - 1
    t[:, C_IOTA] = c + 0 * r
    for level in range(LEVELS):
        w = 1 << level
        low = (r // (2 * w) == c // (2 * w)) & (r // w % 2 == 1) & (c // w % 2 == 0)
        if level == 0:
            t[:, C_M0] = low
        t[:, C_MT + level] = low.T
    return t.reshape(P, C_N * P)


def bucket_rows():
    dist = T - 1 - np.arange(T + P)
    n = np.maximum(dist, 0)
    exact = BUCKETS // 2
    nf = np.maximum(n, 1).astype(np.float32)
    large = exact + (np.log(nf / np.float32(exact)) / np.float32(math.log(1024 / exact))
                     * np.float32(BUCKETS - exact)).astype(np.int32)
    b = np.where(n < exact, n, np.minimum(large, BUCKETS - 1))
    return (b[None, :] == np.arange(BUCKETS)[:, None]).astype(np.float32)


class Tables:

    def __init__(self, nc, outer):
        self.nc = nc
        self.held = []
        self.bank = [outer.enter_context(nc.psum_tensor(f"bank{i}", [P, T], F32)) for i in range(8)]
        self.cst = outer.enter_context(nc.sbuf_tensor("cst", [P, C_N * P], F32))
        self.vec = outer.enter_context(nc.sbuf_tensor("vec", [P, V_N], F32))

    def sem(self, name):
        self.held.append(self.nc.alloc_semaphore(name=name))
        return self.held[-1]

    def free_semaphores(self):
        self.nc.clear_and_free_semaphores(self.held)
        self.nc.all_engine_barrier()
        self.held = []

    def c(self, k, n=1):
        return self.cst[:, k * P:(k + n) * P]

    def per_block(self, k):
        return self.cst[:, k * P:(k + 1) * P].unsqueeze(1).to_broadcast([P, NB, P])


def blocks(ap):
    return ap.rearrange("p (b c) -> p b c", b=NB)


def pairs(eng, cuts, body):
    for k, (a, b) in enumerate(zip(cuts, cuts[1:])):
        if b - a == 1:
            body(a, k)
        else:
            with eng.Fori(a, b) as u:
                body(u, k)


def project_stage(t, tag, w_d, n, source, gain, hi, lo, dest, add=None, side=None, y=None, fetch=None):
    nc = t.nc
    loaded = [t.sem(f"{tag}_loaded{s}") for s in range(2)]
    w_high, w_low, summed, stored, high, low, low_odd = (
        t.sem(f"{tag}_{k}") for k in ("w_high", "w_low", "summed", "stored", "high", "low", "low_odd"))
    side = side(stored) if side else {}
    if fetch:
        arrived, tables_in = [t.sem(f"{tag}_arrived{c}") for c in range(DC // 2)], t.sem(f"{tag}_tables_in")
        norm_cols = slice(0, (C_ONES + 1) * P)
    plain = ((0, 1, n // 2), lambda u, s, k: None)
    if gain is not None:
        squared, added, rooted, inverted, normed = (
            t.sem(f"{tag}_{k}") for k in ("squared", "added", "rooted", "inverted", "normed"))
    with ExitStack() as ctx:
        raw = ctx.enter_context(nc.sbuf_tensor(f"{tag}_raw", [P, 2, D], F32))
        whi = ctx.enter_context(nc.sbuf_tensor(f"{tag}_whi", [P, 2, D], F32R))
        wlo = ctx.enter_context(nc.sbuf_tensor(f"{tag}_wlo", [P, 2, D], F32R))
        if gain is not None:
            if y is None:
                y = ctx.enter_context(nc.sbuf_tensor(f"{tag}_y", [P, DC, T], F32))
            root = ctx.enter_context(nc.sbuf_tensor(f"{tag}_root", [P, 2, T], F32))
        else:
            y = source
        with nc.Block() as block:

            @block.sync
            def _(sp):
                def load(u, k):
                    for s in range(2):
                        if k:
                            sp.wait_ge(w_low, 2 * u + s - 1)
                        sp.dma_start(raw[:, s, :], w_d[2 * u + s]).then_inc(loaded[s], 16)
                if fetch:
                    x_d, cst_d, vec_d = fetch
                    sp.dma_start(t.cst[:, norm_cols], cst_d[:, norm_cols]).then_inc(tables_in, 16)
                    for c in range(DC // 2):
                        sp.dma_start(source[:, 2 * c:2 * c + 2, :], x_d[:, 2 * c:2 * c + 2, :]).then_inc(arrived[c], 16)
                    sp.dma_start(t.vec[:], vec_d).then_inc(tables_in, 16)
                pairs(sp, (0, 1, n // 2), load)
                if fetch:
                    rest = slice(norm_cols.stop, C_N * P)
                    sp.dma_start(t.cst[:, rest], cst_d[:, rest]).then_inc(tables_in, 16)
                    sp.wait_ge(tables_in, 48)

            @block.scalar
            def _(act):
                a = nc.scalar.activation
                cuts, other = side.get("scalar", plain)

                def w_split(u, s, first):
                    act.wait_ge(loaded[s], 16 * (u + 1))
                    if not first:
                        act.wait_ge(summed, 2 * u + s - 1)
                    a(whi[:, s, :], raw[:, s, :], ACT.Copy).then_inc(w_high, 1)

                def store(u, s):
                    if add is None:
                        act.wait_ge(summed, 2 * u + s + 1)
                        a(dest(2 * u + s), t.bank[s][:], ACT.Copy).then_inc(stored, 1)

                def pair(u, k):
                    for s in range(2):
                        w_split(u, s, k == 0)
                        if k:
                            store(u - 1, s)
                        other(u, s, k)
                    if k == 0:
                        if gain is not None:
                            if fetch:
                                act.wait_ge(tables_in, 32)
                            act.wait_ge(added, 1)
                            a(root[:, 0, :], t.bank[7][:], ACT.Ln, scale=1.0 / D,
                              bias=t.vec[:, V_EPS:V_EPS + 1]).then_inc(rooted, 1)
                            act.wait_ge(rooted, 1)
                            a(root[:, 1, :], root[:, 0, :], ACT.Exp, scale=-0.5).then_inc(inverted, 1)
                        for c in range(DC):
                            if gain is not None:
                                act.wait_ge(normed, c + 1)
                            a(hi[:, c, :], y[:, c, :], ACT.Copy).then_inc(high, 1)

                if gain is not None:
                    for c in range(DC):
                        if fetch and c % 2 == 0:
                            act.wait_ge(arrived[c // 2], 16)
                        a(y[:, c, :], source[:, c, :], ACT.Square).then_inc(squared, 1)
                pairs(act, cuts, pair)
                store(n // 2 - 1, 0)
                store(n // 2 - 1, 1)

            @block.vector
            def _(dve):
                cuts, other = side.get("vector", plain)

                def minus(out, whole, part, done):
                    nc.vector.tensor_tensor(out, whole, part.bitcast(F32), ALU.subtract).then_inc(done, 1)

                def w_rest(u, s):
                    dve.wait_ge(w_high, 2 * u + s + 1)
                    minus(wlo[:, s, :], raw[:, s, :], whi[:, s, :], w_low)

                def store(u, s):
                    if add is not None:
                        dve.wait_ge(summed, 2 * u + s + 1)
                        nc.vector.tensor_tensor(dest(2 * u + s), add(2 * u + s), t.bank[s][:],
                                                ALU.add).then_inc(stored, 1)

                def pair(u, k):
                    for s in range(2):
                        w_rest(u, s)
                        if k:
                            store(u - 1, s)
                        other(u, s, k)
                    if k == 0:
                        if gain is not None:
                            dve.wait_ge(inverted, 1)
                        for c in range(DC):
                            if gain is not None:
                                nc.vector.scalar_tensor_tensor(
                                    y[:, c, :], source[:, c, :], t.vec[:, gain + c:gain + c + 1], root[:, 1, :],
                                    ALU.mult, ALU.mult).then_inc(normed, 1)
                            if c % 2:
                                dve.wait_ge(high, c)
                                minus(lo[:, c - 1, :], y[:, c - 1, :], hi[:, c - 1, :], low)

                pairs(dve, cuts, pair)
                store(n // 2 - 1, 0)
                store(n // 2 - 1, 1)

            @block.gpsimd
            def _(pool):
                for c in range(1, DC, 2):
                    pool.wait_ge(high, c + 1)
                    nc.gpsimd.tensor_tensor(lo[:, c, :], y[:, c, :], hi[:, c, :].bitcast(F32),
                                            ALU.subtract).then_inc(low_odd, 1)

            @block.tensor
            def _(pe):
                mm = nc.tensor.matmul
                cuts, other = side.get("tensor", plain)

                def pair(u, k):
                    for s in range(2):
                        pe.wait_ge(w_low, 2 * u + s + 1)
                        if k:
                            pe.wait_ge(stored, 2 * u + s - 1)
                        for c in range(DC):
                            w = slice(c * P, (c + 1) * P)
                            if k == 0 and s == 0:
                                pe.wait_ge(low_odd if c % 2 else low, c // 2 + 1)
                            mm(t.bank[s][:], whi[:, s, w], hi[:, c, :], start=c == 0, stop=False)
                            mm(t.bank[s][:], whi[:, s, w], lo[:, c, :], start=False, stop=False)
                            last = mm(t.bank[s][:], wlo[:, s, w], hi[:, c, :], start=False, stop=c == DC - 1)
                        last.then_inc(summed, 1)
                        other(u, s, k)

                if gain is not None:
                    if fetch:
                        pe.wait_ge(tables_in, 32)
                    for c in range(DC):
                        pe.wait_ge(squared, c + 1)
                        last = mm(t.bank[7][:], t.c(C_ONES), y[:, c, :], start=c == 0, stop=c == DC - 1)
                    last.then_inc(added, 1)
                pairs(pe, cuts, pair)


def convolution(t, proj, conv, sq, root):
    nc = t.nc
    taps, silu, squared, sumsq, rooted, inverted, normed = (
        t.sem("conv_" + k) for k in ("taps", "silu", "squared", "sumsq", "rooted", "inverted", "normed"))
    v = t.vec
    NQKV, NPAIR = QKV_T // 2, NPROJ // 2

    def side(stored):
        def vector(u, s, k):
            if k in (1, 2):
                j = 2 * (u - 1) + s
                for tap in range(CONV):
                    weight = v[:, bass.ds(V_CONV + j * CONV + tap, 1)]
                    if tap == 0:
                        nc.vector.wait_ge(stored, j + 1)
                        nc.vector.tensor_scalar(conv[:, j, :], proj[:, j, 0:T], weight, None,
                                                ALU.mult).then_inc(taps, 1)
                    else:
                        nc.vector.wait_ge(taps, CONV * j + tap)
                        nc.vector.scalar_tensor_tensor(conv[:, j, :], proj[:, j, tap:tap + T], weight, conv[:, j, :],
                                                       ALU.mult, ALU.add).then_inc(taps, 1)
            elif k == 3:
                j = 2 * (u - NQKV - 1) + s
                nc.vector.wait_ge(rooted, j + 1)
                nc.vector.reciprocal(root[:, s, :], root[:, s, :]).then_inc(inverted, 1)
                nc.vector.wait_ge(inverted, j + 1)
                nc.vector.scalar_tensor_tensor(conv[:, j, :], conv[:, j, :], v[:, bass.ds(V_QK + j, 1)],
                                               root[:, s, :], ALU.mult, ALU.mult).then_inc(normed, 1)

        def scalar(u, s, k):
            if k in (2, 3, 4):
                j = 2 * (u - 2) + s
                nc.scalar.wait_ge(taps, CONV * (j + 1))
                nc.scalar.activation(conv[:, j, :], conv[:, j, :], ACT.Silu).then_inc(silu, 1)
                if k == 2:
                    nc.scalar.wait_ge(silu, j + 1)
                    nc.scalar.activation(sq[:, j, :], conv[:, j, :], ACT.Square).then_inc(squared, 1)
            if k in (4, 5):
                j = 2 * (u - 1) + s
                nc.scalar.wait_ge(stored, j + 1)
                z = proj[:, j, PAD:PAD + T]
                nc.scalar.activation(z, z, ACT.Silu).then_inc(silu, 1)
            if k in (4, 5, 6):
                j = 2 * (u - NQKV - 1) + s
                nc.scalar.wait_ge(sumsq, j + 1)
                if k != 4:
                    nc.scalar.wait_ge(normed, j - 1)
                nc.scalar.activation(root[:, s, :], t.bank[2 + s][:], ACT.Sqrt,
                                     bias=v[:, V_EPS:V_EPS + 1]).then_inc(rooted, 1)

        def tensor(u, s, k):
            if k in (2, 3):
                j = 2 * (u - NQKV) + s
                nc.tensor.wait_ge(squared, j + 1)
                if k == 3:
                    nc.tensor.wait_ge(rooted, j - 1)
                nc.tensor.matmul(t.bank[2 + s][:], t.c(C_ONES), sq[:, j, :], start=True,
                                 stop=True).then_inc(sumsq, 1)

        return {"vector": ((0, 1, NQKV, NQKV + 1, NPAIR), vector),
                "scalar": ((0, 1, 2, NQKV, NQKV + 1, NQKV + 2, NQKV + 3, NPAIR), scalar),
                "tensor": ((0, 1, NQKV, NQKV + 1, NPAIR - 1, NPAIR), tensor)}
    return side


def delta_stage(t, proj, conv, mix, wqi, wqi_d):
    nc = t.nc
    s = {n: t.sem("gdn_" + n) for n in (
        "chain", "ab_t", "ab", "exps", "u1", "log",
        "g", "beta", "cums", "g_col", "decays", "beg", "gl", "grow", "dif", "exp3", "dmask", "tiles_t", "kk",
        "taken", "qk", "a", "a_t", "at", "prep", "mt", "x", "xs", "tx", "level", "uw_t", "u", "w", "zero",
        "ws", "vnew", "out", "o_copy", "ds", "state", "osq", "ossq", "olog", "oinv", "mixed",
        "wqi", "lsq", "mean", "centred", "csq", "lsum", "llog", "linv", "latents", "kin")}
    v = t.vec
    with ExitStack() as ctx:
        def sb(name, shape):
            return ctx.enter_context(nc.sbuf_tensor("gdn_" + name, shape, F32))

        keyed = sb("keyed", [P, 2 * H, T])
        sq = sb("sq", [P, 2 * H, T])
        ab = sb("ab", [P, NB, 8])
        small = sb("small", [P, 16, 16])
        ghalf = sb("ghalf", [P, 2, 16])
        qeg = sb("qeg", [P, H, T])
        at = sb("at", [P, H, T])
        attn = sb("attn", [P, H, T])
        mt_u = sb("mt_u", [P, H, T])
        x_w = sb("x_w", [P, H, T])
        tmp = sb("tmp", [P, 8, T])
        qk = conv[:, 0:2 * H]
        kbg, kdec, vb = keyed[:, 0:H], keyed[:, H:2 * H], conv[:, 2 * H:3 * H]
        ti, tt = sq[:, 0:H], sq[:, H:2 * H]
        gl, dif, pos, neg, eg, dn, dt = (tmp[:, i, :] for i in range(7))
        am = (tmp[:, 7, :], x_w[:, 0, :])
        log_inv = [tmp[:, i, :] for i in (4, 5, 7)]
        csq = tmp[:, 6, :]
        lsq = at
        latent = [proj[:, CQ0 + i, PAD:PAD + T] for i in range(4)]
        keys_i = proj[:, KI0, PAD:PAD + T]
        sm = [small[:, i, :] for i in range(16)]
        xa, nx, z, u1, lnu, eq, rat, sp_, g, ebb, beta, gcol, eg_col, egam, beg, ea = sm

        def by_block(ap):
            return lambda h: ap.rearrange("p (b h) -> p b h", h=H)[:, :, h:h + 1].to_broadcast([P, NB, P])

        with nc.Block() as block:

            @block.sync
            def _(sp):
                sp.dma_start(wqi[:], wqi_d).then_inc(s["wqi"], 16)
                sp.wait_ge(s["wqi"], 16)

            @block.vector
            def _(dve):
                chain = [0]

                def link(ins):
                    chain[0] += 1
                    ins.then_inc(s["chain"], 1)
                    dve.wait_ge(s["chain"], chain[0])

                tt_, ts = nc.vector.tensor_tensor, nc.vector.tensor_scalar
                stt = nc.vector.scalar_tensor_tensor
                dve.wait_ge(s["ab_t"], 1)
                link(nc.vector.tensor_copy(ab[:], blocks(t.bank[7][:])[:, :, 0:8]))
                r3 = lambda ap: ap.rearrange("p (b h) -> p b h", h=H)
                link(tt_(r3(xa), ab[:, :, 0:H], v[:, V_DTB:V_DTB + H].unsqueeze(1).to_broadcast([P, NB, H]), ALU.add))
                link(ts(nx, xa, -1.0, None, ALU.mult))
                tt_(nx, nx, xa, ALU.min).then_inc(s["ab"], 1)
                dve.wait_ge(s["exps"], 3)
                ts(u1, z, 1.0, None, ALU.add).then_inc(s["u1"], 1)
                dve.wait_ge(s["u1"], 1)
                link(ts(eq, u1, 1.0, None, ALU.is_equal))
                link(stt(rat, u1, -1.0, eq, ALU.add, ALU.add))
                link(nc.vector.reciprocal(rat, rat))
                link(tt_(rat, rat, z, ALU.mult))
                dve.wait_ge(s["log"], 1)
                link(tt_(lnu, lnu, eq, ALU.add))
                link(tt_(rat, rat, lnu, ALU.mult))
                link(stt(sp_, xa, 0.0, rat, ALU.max, ALU.add))
                tt_(r3(g), r3(sp_), ea[:, 0:H].unsqueeze(1).to_broadcast([P, NB, H]), ALU.mult).then_inc(s["chain"], 1)
                chain[0] += 1
                dve.wait_ge(s["chain"], chain[0])
                ts(g, g, -1.0, None, ALU.mult).then_inc(s["g"], 1)
                link(ts(beta, ebb, 1.0, None, ALU.add))
                nc.vector.reciprocal(beta, beta).then_inc(s["beta"], 1)
                dve.wait_ge(s["cums"], 1)
                nc.vector.tensor_copy(gcol, t.bank[6][:, 0:16]).then_inc(s["g_col"], 1)
                dve.wait_ge(s["g_col"], 1)
                link(tt_(egam, t.bank[6][:, 16:32], gcol, ALU.subtract))
                nc.vector.tensor_copy(ghalf[:], t.bank[6][:, 32:64].rearrange("p (a b) -> p a b", a=2)).then_inc(s["g_col"], 1)
                dve.wait_ge(s["decays"], 3)
                tt_(beg, beta, eg_col, ALU.mult).then_inc(s["beg"], 1)
                dve.wait_ge(s["beg"], 1)
                def spread(h):
                    tt_(blocks(gl), t.per_block(C_CUM), by_block(g)(h), ALU.mult).then_inc(s["gl"], 1)

                def differences(h):
                    dve.wait_ge(s["grow"], h + 1)
                    link(tt_(blocks(dif), blocks(t.bank[0][:]), by_block(gcol)(h), ALU.subtract))
                    ts(pos, dif, 0.0, None, ALU.max).then_inc(s["dif"], 1)
                    ts(neg, dif, 0.0, None, ALU.min).then_inc(s["dif"], 1)

                def first_level(h):
                    link(tt_(blocks(ti[:, h, :]), blocks(am[h % 2]), t.per_block(C_M0), ALU.mult))
                    link(tt_(blocks(ti[:, h, :]), t.per_block(C_ID), blocks(ti[:, h, :]), ALU.subtract))
                    dve.wait_ge(s["at"], h + 1)
                    link(tt_(blocks(tt[:, h, :]), blocks(at[:, h, :]), t.per_block(C_MT), ALU.mult))
                    tt_(blocks(tt[:, h, :]), t.per_block(C_ID), blocks(tt[:, h, :]), ALU.subtract).then_inc(s["prep"], 1)

                spread(0)
                for h in range(H):
                    if h:
                        dve.wait_ge(s["exp3"], 3 * h)
                    differences(h)
                    dve.wait_ge(s["tiles_t"], 2 * (h + 1))
                    tt_(blocks(kbg[:, h, :]), blocks(t.bank[1][:]), by_block(beg)(h), ALU.mult)
                    tt_(blocks(kdec[:, h, :]), blocks(t.bank[1][:]), by_block(egam)(h), ALU.mult)
                    tt_(blocks(vb[:, h, :]), blocks(t.bank[2][:]), by_block(beta)(h), ALU.mult).then_inc(s["taken"], 1)
                    if h + 1 < H:
                        spread(h + 1)
                    if h:
                        first_level(h - 1)
                    dve.wait_ge(s["exp3"], 3 * (h + 1))
                    tt_(qeg[:, h, :], qk[:, h, :], eg, ALU.mult)
                    link(tt_(blocks(dn), blocks(dn), t.per_block(C_STRICT), ALU.mult))
                    link(tt_(blocks(dn), blocks(dn), by_block(beta)(h), ALU.mult))
                    link(tt_(blocks(dt), blocks(dt), t.per_block(C_CUM), ALU.mult))
                    dve.wait_ge(s["kk"], 2 * (h + 1))
                    tt_(am[h % 2], t.bank[3][:], dn, ALU.mult).then_inc(s["a"], 1)
                    tt_(attn[:, h, :], t.bank[4][:], dt, ALU.mult).then_inc(s["qk"], 1)
                    dve.wait_ge(s["a"], h + 1)
                first_level(H - 1)
                dve.wait_ge(s["prep"], H)
                for level in range(1, LEVELS):
                    for h in range(H):
                        if level > 1:
                            dve.wait_ge(s["x"], H * (level - 2) + h + 1)
                        tt_(blocks(mt_u[:, h, :]), blocks(at[:, h, :]), t.per_block(C_MT + level),
                            ALU.mult).then_inc(s["mt"], 1)
                    for h in range(H):
                        dve.wait_ge(s["tx"], H * (level - 1) + h + 1)
                        if level < LEVELS - 1:
                            tt_(ti[:, h, :], ti[:, h, :], t.bank[4 + h % 2][:], ALU.subtract)
                        tt_(tt[:, h, :], tt[:, h, :], t.bank[6 + h % 2][:], ALU.subtract).then_inc(s["level"], 1)
                for h in range(H):
                    dve.wait_ge(s["uw_t"], h + 1)
                    nc.vector.tensor_copy(mt_u[:, h, :], t.bank[h % 2][:]).then_inc(s["u"], 1)
                states, vn, dec = (tmp[:, 0, :], tmp[:, 3, :]), tmp[:, 1, :], tmp[:, 2, :]
                nc.vector.memset(states[0], 0.0).then_inc(s["zero"], 1)
                dve.wait_ge(s["zero"], 1)
                dve.wait_ge(s["u"], H)
                u4 = mt_u[:].rearrange("p h (b c) -> p h b c", b=NB)
                for n in range(NCH):
                    b, rows = n // 2, slice(CHUNK * (n % 2), CHUNK * (n % 2) + CHUNK)
                    state, after = states[n % 2], states[(n + 1) % 2]
                    dve.wait_ge(s["ws"], n + 1)
                    tt_(vn[rows, :].rearrange("p (h c) -> p h c", h=H), u4[rows, :, b, :],
                        t.bank[4][rows, :].rearrange("p (h c) -> p h c", h=H), ALU.subtract).then_inc(s["vnew"], 1)
                    decay = ghalf[:, n % 2, b * H:(b + 1) * H].unsqueeze(2).to_broadcast([P, H, P])
                    link(tt_(dec.rearrange("p (h c) -> p h c", h=H), state.rearrange("p (h c) -> p h c", h=H),
                             decay, ALU.mult))
                    dve.wait_ge(s["ds"], n + 1)
                    tt_(after, dec, t.bank[6][:], ALU.add).then_inc(s["state"], 1)
                    dve.wait_ge(s["state"], n + 1)
                    if n == 0:
                        dve.wait_ge(s["mean"], 1)
                        stt(keys_i, t.bank[0][:], -1.0 / IDIM, keys_i, ALU.mult, ALU.add).then_inc(s["centred"], 1)
                    if n in (5, 6):
                        dve.wait_ge(s["linv"], n - 4)
                        for i in (2 * n - 10, 2 * n - 9):
                            stt(latent[i], latent[i], v[:, V_QN + i:V_QN + i + 1], log_inv[n - 5],
                                ALU.mult, ALU.mult).then_inc(s["latents"], 1)
                    if n == 7:
                        dve.wait_ge(s["linv"], 3)
                        stt(keys_i, keys_i, v[:, V_IG:V_IG + 1], log_inv[2], ALU.mult, ALU.mult).then_inc(s["kin"], 1)
                        dve.wait_ge(s["kin"], 1)
                        ts(keys_i, keys_i, v[:, V_IB:V_IB + 1], None, ALU.add).then_inc(s["kin"], 1)
                for h in range(H):
                    dve.wait_ge(s["oinv"], h + 1)
                    link(stt(qeg[:, h, :], qk[:, h, :], v[:, V_GDN:V_GDN + 1], tmp[:, 4 + h, :], ALU.mult, ALU.mult))
                    tt_(mix[:, h, :], qeg[:, h, :], proj[:, Z0 + h, PAD:PAD + T], ALU.mult).then_inc(s["mixed"], 1)

            @block.scalar
            def _(act):
                a = nc.scalar.activation
                a(ea[:, 0:H], v[:, V_ALOG:V_ALOG + H], ACT.Exp).then_inc(s["exps"], 1)
                act.wait_ge(s["ab"], 1)
                a(z, nx, ACT.Exp).then_inc(s["exps"], 1)
                a(ebb.rearrange("p (b h) -> p b h", h=H), ab[:, :, H:2 * H], ACT.Exp, scale=-1.0).then_inc(s["exps"], 1)
                act.wait_ge(s["u1"], 1)
                a(lnu, u1, ACT.Ln).then_inc(s["log"], 1)
                act.wait_ge(s["g_col"], 2)
                a(eg_col, gcol, ACT.Exp).then_inc(s["decays"], 1)
                a(egam, egam, ACT.Exp).then_inc(s["decays"], 1)
                a(ghalf[:], ghalf[:], ACT.Exp).then_inc(s["decays"], 1)
                def turn(h):
                    act.wait_ge(s["a_t"], h + 1)
                    a(at[:, h, :], t.bank[5][:], ACT.Copy).then_inc(s["at"], 1)

                for h in range(H):
                    act.wait_ge(s["dif"], 2 * h + 1)
                    if h:
                        act.wait_ge(s["qk"], h)
                    a(eg, t.bank[0][:], ACT.Exp).then_inc(s["exp3"], 1)
                    act.wait_ge(s["dif"], 2 * (h + 1))
                    a(dn, pos, ACT.Exp, scale=-1.0).then_inc(s["exp3"], 1)
                    a(dt, neg, ACT.Exp).then_inc(s["exp3"], 1)
                    if h:
                        turn(h - 1)
                turn(H - 1)
                for level in range(1, LEVELS):
                    for h in range(H):
                        act.wait_ge(s["x"], H * (level - 1) + h + 1)
                        a(x_w[:, h, :], t.bank[h][:], ACT.Copy).then_inc(s["xs"], 1)
                for h in range(H):
                    act.wait_ge(s["uw_t"], h + 1)
                    a(x_w[:, h, :], t.bank[2 + h % 2][:], ACT.Copy).then_inc(s["w"], 1)
                act.wait_ge(s["mt"], H * (LEVELS - 1))
                for i in range(4):
                    a(lsq[:, i, :], latent[i], ACT.Square).then_inc(s["lsq"], 1)
                for n in range(NCH):
                    act.wait_ge(s["out"], n + 1)
                    a(qk[:, 0:H, n * CHUNK:(n + 1) * CHUNK],
                      t.bank[5][:, 0:H * CHUNK].rearrange("p (h c) -> p h c", h=H), ACT.Copy).then_inc(s["o_copy"], 1)
                    if n == 1:
                        act.wait_ge(s["centred"], 1)
                        a(csq, keys_i, ACT.Square).then_inc(s["csq"], 1)
                    if n in (2, 3, 4):
                        k, width = n - 2, (RANK, RANK, IDIM)[n - 2]
                        act.wait_ge(s["lsum"], k + 1)
                        a(log_inv[k], t.bank[1 + k][:], ACT.Ln, scale=1.0 / width,
                          bias=v[:, V_EPS:V_EPS + 1]).then_inc(s["llog"], 1)
                    if n == 4:
                        for k in range(3):
                            act.wait_ge(s["llog"], k + 1)
                            a(log_inv[k], log_inv[k], ACT.Exp, scale=-0.5).then_inc(s["linv"], 1)
                act.wait_ge(s["o_copy"], NCH)
                for h in range(H):
                    a(sq[:, h, :], qk[:, h, :], ACT.Square).then_inc(s["osq"], 1)
                act.wait_ge(s["latents"], 4)
                act.wait_ge(s["kin"], 1)
                for h in range(H):
                    act.wait_ge(s["ossq"], h + 1)
                    a(tmp[:, 4 + h, :], t.bank[h][:], ACT.Ln, scale=1.0 / P,
                      bias=v[:, V_EPS:V_EPS + 1]).then_inc(s["olog"], 1)
                for h in range(H):
                    act.wait_ge(s["olog"], h + 1)
                    a(tmp[:, 4 + h, :], tmp[:, 4 + h, :], ACT.Exp, scale=-0.5).then_inc(s["oinv"], 1)

            @block.tensor
            def _(pe):
                mm, tr = nc.tensor.matmul, nc.tensor.transpose
                ident, ones = t.c(C_ID), t.c(C_ONES)
                for b in range(NB):
                    last = tr(t.bank[7][:, b * P:(b + 1) * P], proj[:, AB0, PAD + b * P:PAD + (b + 1) * P], ident)
                last.then_inc(s["ab_t"], 1)
                pe.wait_ge(s["g"], 1)
                mm(t.bank[6][:, 0:16], t.c(C_CUM), g, start=True, stop=True)
                mm(t.bank[6][:, 16:32], t.c(C_SAME), g, start=True, stop=True)
                mm(t.bank[6][:, 32:48], t.c(C_HALF0), g, start=True, stop=True)
                mm(t.bank[6][:, 48:64], t.c(C_HALF0 + 1), g, start=True, stop=True).then_inc(s["cums"], 1)
                def row(h):
                    pe.wait_ge(s["gl"], h + 1)
                    if h:
                        pe.wait_ge(s["exp3"], 3 * h - 2)
                    mm(t.bank[0][:], ones, gl, start=True, stop=True).then_inc(s["grow"], 1)

                def products(h):
                    q, k = qk[:, h, :], qk[:, H + h, :]
                    if h:
                        pe.wait_ge(s["taken"], h)
                    for src, bank in ((k, 1), (conv[:, 2 * H + h, :], 2)):
                        for b in range(NB):
                            last = tr(t.bank[bank][:, b * P:(b + 1) * P], src[:, b * P:(b + 1) * P], ident)
                        last.then_inc(s["tiles_t"], 1)
                    if h:
                        pe.wait_ge(s["qk"], h)
                    for left, right, bank in ((k, k, 3), (k, q, 4)):
                        for b in range(NB):
                            w = slice(b * P, (b + 1) * P)
                            last = mm(t.bank[bank][:, w], left[:, w], right[:, w], start=True, stop=True)
                        last.then_inc(s["kk"], 1)

                row(0)
                products(0)
                for h in range(H):
                    if h + 1 < H:
                        row(h + 1)
                        products(h + 1)
                    pe.wait_ge(s["a"], h + 1)
                    if h:
                        pe.wait_ge(s["at"], h)
                    for b in range(NB):
                        last = tr(t.bank[5][:, b * P:(b + 1) * P], am[h % 2][:, b * P:(b + 1) * P], ident)
                    last.then_inc(s["a_t"], 1)
                pe.wait_ge(s["prep"], H)
                for level in range(1, LEVELS):
                    done = H * (level - 1)
                    for h in range(H):
                        pe.wait_ge(s["mt"], done + h + 1)
                        if level > 1:
                            pe.wait_ge(s["level"], done - H + h + 1)
                        for b in range(NB):
                            w = slice(b * P, (b + 1) * P)
                            last = mm(t.bank[h][:, w], mt_u[:, h, w], ti[:, h, w], start=True, stop=True)
                        last.then_inc(s["x"], 1)
                    for h in range(H):
                        pe.wait_ge(s["xs"], done + h + 1)
                        if h >= 2:
                            pe.wait_ge(s["level"], done + h - 1)
                        for b in range(NB):
                            w = slice(b * P, (b + 1) * P)
                            if level < LEVELS - 1:
                                mm(t.bank[4 + h % 2][:, w], tt[:, h, w], x_w[:, h, w], start=True, stop=True)
                            last = mm(t.bank[6 + h % 2][:, w], x_w[:, h, w], tt[:, h, w], start=True, stop=True)
                        last.then_inc(s["tx"], 1)
                for h in range(H):
                    pe.wait_ge(s["level"], H * (LEVELS - 2) + h + 1)
                    if h == 0:
                        pe.wait_ge(s["xs"], H * (LEVELS - 1))
                    if h >= 2:
                        pe.wait_ge(s["u"], h - 1)
                        pe.wait_ge(s["w"], h - 1)
                    for b in range(NB):
                        w = slice(b * P, (b + 1) * P)
                        mm(t.bank[h % 2][:, w], tt[:, h, w], vb[:, h, w], start=True, stop=True)
                        last = mm(t.bank[2 + h % 2][:, w], kbg[:, h, w], tt[:, h, w], start=True, stop=True)
                    last.then_inc(s["uw_t"], 1)
                states, vn = (tmp[:, 0, :], tmp[:, 3, :]), tmp[:, 1, :]
                pe.wait_ge(s["zero"], 1)
                pe.wait_ge(s["w"], H)
                for n in range(NCH):
                    b, rows = n // 2, slice(CHUNK * (n % 2), CHUNK * (n % 2) + CHUNK)
                    cols = slice(n * CHUNK, (n + 1) * CHUNK)
                    state = states[n % 2]
                    if n:
                        pe.wait_ge(s["state"], n)
                    for h in range(H):
                        last = mm(t.bank[4][rows, h * P:(h + 1) * P], x_w[:, h, cols], state[:, h * P:(h + 1) * P],
                                  start=True, stop=True)
                    last.then_inc(s["ws"], 1)
                    pe.wait_ge(s["vnew"], n + 1)
                    for h in range(H):
                        last = mm(t.bank[6][:, h * P:(h + 1) * P], kdec[rows, h, b * P:(b + 1) * P],
                                  vn[rows, h * P:(h + 1) * P], start=True, stop=True)
                    last.then_inc(s["ds"], 1)
                    if n:
                        pe.wait_ge(s["o_copy"], n)
                    for h in range(H):
                        o = t.bank[5][:, h * CHUNK:(h + 1) * CHUNK]
                        mm(o, state[:, h * P:(h + 1) * P], qeg[:, h, cols], start=True, stop=False)
                        last = mm(o, vn[rows, h * P:(h + 1) * P], attn[rows, h, cols], start=False, stop=True)
                    last.then_inc(s["out"], 1)
                    if n == 0:
                        pe.wait_ge(s["u"], H)
                        mm(t.bank[0][:], t.c(C_SAME), keys_i, start=True, stop=True).then_inc(s["mean"], 1)
                    if n in (1, 2):
                        pe.wait_ge(s["lsq"], 2 * n)
                        mm(t.bank[n][:], ones, lsq[:, 2 * n - 2, :], start=True, stop=False)
                        mm(t.bank[n][:], ones, lsq[:, 2 * n - 1, :], start=False, stop=True).then_inc(s["lsum"], 1)
                    if n == 3:
                        pe.wait_ge(s["csq"], 1)
                        mm(t.bank[3][:], t.c(C_SAME), csq, start=True, stop=True).then_inc(s["lsum"], 1)
                pe.wait_ge(s["centred"], 1)
                pe.wait_ge(s["llog"], 3)
                for h in range(H):
                    pe.wait_ge(s["osq"], h + 1)
                    mm(t.bank[h][:], ones, sq[:, h, :], start=True, stop=True).then_inc(s["ossq"], 1)


def sparse_stage(t, proj, mix, wqi, wq_d, wkv_d, rel_d, buckets_d, strip_d):
    nc = t.nc
    s = {n: t.sem("dsa_" + n) for n in (
        "chain", "wq", "wkv", "rel", "w_t", "w", "up", "up_out", "v_up", "v_out", "strip", "strip_s", "strip_out", "slid", "flip",
        "bias", "bias_m", "dots", "relu", "score", "fenced", "masked", "logits", "centre", "peak", "exp", "prob",
        "prob_t", "turned", "pv", "mixed")}
    v = t.vec
    NUP = H + IH // 2 + H
    QI0, K0 = H, H + IH // 2
    order = list(range(QI0, K0)) + list(range(QI0)) + list(range(K0, NUP))
    dots = (NB - 1) * IH
    W = T + P
    ROUNDS = TOPK // 8
    assert ROUNDS == IH == 4 * H
    with ExitStack() as ctx:
        def sb(name, shape):
            return ctx.enter_context(nc.sbuf_tensor("dsa_" + name, shape, F32))

        wq = sb("wq", [P, 2, H * P])
        wkv = sb("wkv", [P, 2, 2, H * P])
        rel, buckets, strip = sb("rel", [BUCKETS, H]), sb("buckets", [BUCKETS, W]), sb("strip", [H, W])
        lat = proj[:, CQ0:CQ0 + 4, PAD:PAD + T]
        kin = proj[:, KI0, PAD:PAD + T]
        slid = sb("slid", [P, H, T])
        up = sb("up", [P, NUP, T])
        vt = sb("vt", [P, NB, H * P])
        bias = sb("bias", [P, H, T])
        w_idx = sb("w_idx", [P, NB, IH])
        relu = sb("relu", [P, 2, T])
        score = sb("score", [P, NB, T])
        best = sb("best", [P, 8])
        pr, prt = sb("pr", [P, 4, T]), sb("prt", [P, 4, T])
        lg = sb("lg", [P, 4, T])
        peak, total = sb("peak", [P, 4]), sb("total", [P, 4])
        units = [(b, h) for b in range(NB) for h in range(H)]

        with nc.Block() as block:

            @block.sync
            def _(sp):
                sp.dma_start(rel[:], rel_d).then_inc(s["rel"], 16)
                sp.dma_start(buckets[:], buckets_d).then_inc(s["rel"], 16)
                sp.dma_start(wq[:], wq_d).then_inc(s["wq"], 16)
                sp.dma_start(wkv[:], wkv_d).then_inc(s["wkv"], 16)
                sp.wait_ge(s["strip_s"], 2)
                sp.dma_start(strip_d, strip[:]).then_inc(s["strip_out"], 16)
                sp.wait_ge(s["strip_out"], 16)
                for h in range(H):
                    sp.dma_start(slid[:, h, :], bass.AP(strip_d.tensor, h * W, [[1, P], [1, T]])).then_inc(s["slid"], 16)

            @block.scalar
            def _(act):
                a = nc.scalar.activation
                def take_up(n):
                    act.wait_ge(s["up"], n + 1)
                    a(up[:, order[n], :], t.bank[n % 4][:], ACT.Copy).then_inc(s["up_out"], 1)

                for n in range(IH // 2):
                    take_up(n)
                n = 0
                for b in range(1, NB):
                    S = (b + 1) * P
                    for i in range(IH):
                        act.wait_ge(s["dots"], n + 1)
                        if n >= 2:
                            act.wait_ge(s["score"], n - 1)
                        a(relu[:, n % 2, 0:S], t.bank[n % 4][:, 0:S], ACT.Relu).then_inc(s["relu"], 1)
                        n += 1
                for h in range(H):
                    act.wait_ge(s["flip"], h + 1)
                    a(bias[:, h, :], t.bank[6 + h % 2][:], ACT.Copy).then_inc(s["bias"], 1)
                for n in range(IH // 2, NUP):
                    take_up(n)
                for b in range(NB):
                    act.wait_ge(s["v_up"], b + 1)
                    a(vt[:, b, :], t.bank[4 + b % 2][:], ACT.Copy).then_inc(s["v_out"], 1)

                def exps(u):
                    S = (units[u][0] + 1) * P
                    act.wait_ge(s["peak"], u + 1)
                    if u >= 4:
                        act.wait_ge(s["prob_t"], u - 3)
                    a(pr[:, u % 4, 0:S], lg[:, u % 4, 0:S], ACT.Exp, bias=peak[:, u % 4:u % 4 + 1],
                      accum_out=total[:, u % 4:u % 4 + 1]).then_inc(s["exp"], 1)

                def store(u):
                    b, h = units[u]
                    act.wait_ge(s["pv"], u + 1)
                    a(mix[:, H + h, b * P:(b + 1) * P], t.bank[6 + u % 2][:, 0:P], ACT.Copy).then_inc(s["mixed"], 1)

                exps(0)
                exps(1)
                for u, (b, h) in enumerate(units):
                    S = (b + 1) * P
                    act.wait_ge(s["prob_t"], u + 1)
                    if u >= 4:
                        act.wait_ge(s["pv"], u - 3)
                    a(prt[:, u % 4, 0:S], t.bank[4 + u % 2][:, 0:S], ACT.Copy).then_inc(s["turned"], 1)
                    if u:
                        store(u - 1)
                    if u + 2 < len(units):
                        exps(u + 2)
                store(len(units) - 1)

            @block.gpsimd
            def _(pool):
                for b in range(1, NB):
                    pool.wait_ge(s["score"], b * IH)
                    own = score[:, b, b * P:(b + 1) * P]
                    nc.gpsimd.affine_select(out=own, in_=own, pattern=[[-1, P]], base=0, channel_multiplier=1,
                                            compare_op=ALU.is_ge, fill=OUT_OF_REACH).then_inc(s["fenced"], 1)
                pool.wait_ge(s["bias"], H)
                nc.gpsimd.affine_select(out=bias[:], in_=bias[:], pattern=[[0, H], [-1, T]], base=T - P,
                                        channel_multiplier=1, compare_op=ALU.is_ge, fill=NEG).then_inc(s["bias_m"], 1)

            @block.vector
            def _(dve):
                chain = [0]

                def link(ins):
                    chain[0] += 1
                    ins.then_inc(s["chain"], 1)
                    dve.wait_ge(s["chain"], chain[0])

                tt_, ts = nc.vector.tensor_tensor, nc.vector.tensor_scalar
                stt = nc.vector.scalar_tensor_tensor
                dve.wait_ge(s["w_t"], 1)
                ts(w_idx[:], blocks(t.bank[7][:])[:, :, 8:8 + IH], IH ** -0.5 * IDIM ** -0.5, None, ALU.mult).then_inc(s["w"], 1)
                dve.wait_ge(s["strip"], 1)
                nc.vector.tensor_copy(strip[:, 0:T], t.bank[4][0:H, :]).then_inc(s["strip_s"], 1)
                nc.vector.tensor_copy(strip[:, T:W], t.bank[5][0:H, 0:P]).then_inc(s["strip_s"], 1)
                dve.wait_ge(s["w"], 1)

                def accumulate(b, i):
                    n, S = (b - 1) * IH + i, (b + 1) * P
                    dve.wait_ge(s["relu"], n + 1)
                    if i == 0:
                        ts(score[:, b, 0:S], relu[:, n % 2, 0:S], w_idx[:, b, i:i + 1], None, ALU.mult).then_inc(s["score"], 1)
                    else:
                        dve.wait_ge(s["score"], n)
                        stt(score[:, b, 0:S], relu[:, n % 2, 0:S], w_idx[:, b, i:i + 1], score[:, b, 0:S],
                            ALU.mult, ALU.add).then_inc(s["score"], 1)

                def take_best(b, k):
                    sc = score[:, b, 0:(b + 1) * P]
                    if k == 0:
                        dve.wait_ge(s["fenced"], b)
                    link(nc.vector.max(best[:], sc))
                    link(nc.vector.match_replace(sc, best[:], sc, TAKEN))
                    if k == ROUNDS - 1:
                        ts(sc, sc, TAKEN, NEG, ALU.not_equal, ALU.mult).then_inc(s["masked"], 1)

                def logits(u):
                    b, h = units[u]
                    S, o = (b + 1) * P, (NB - 1 - b) * P
                    l = lg[:, u % 4, 0:S]
                    if u == 0:
                        dve.wait_ge(s["bias_m"], 1)
                    if b and h == 0:
                        dve.wait_ge(s["masked"], b)
                    dve.wait_ge(s["logits"], u + 1)
                    if u >= 4:
                        dve.wait_ge(s["exp"], u - 3)
                    link(stt(l, t.bank[u % 4][:, 0:S], P ** -0.5, bias[:, h, o:o + S], ALU.mult, ALU.add))
                    if b:
                        link(tt_(l, l, score[:, b, 0:S], ALU.add))
                    nc.vector.tensor_reduce(peak[:, u % 4:u % 4 + 1], l, AX.X, ALU.max, negate=True).then_inc(s["peak"], 1)

                def probabilities(u):
                    S = (units[u][0] + 1) * P
                    r = total[:, u % 4:u % 4 + 1]
                    dve.wait_ge(s["exp"], u + 1)
                    link(nc.vector.reciprocal(r, r))
                    ts(pr[:, u % 4, 0:S], pr[:, u % 4, 0:S], r, None, ALU.mult).then_inc(s["prob"], 1)

                for i in range(IH):
                    accumulate(1, i)
                for b in range(2, NB):
                    for i in range(IH):
                        accumulate(b, i)
                        take_best(b - 1, i)
                for k in range(ROUNDS):
                    take_best(NB - 1, k)
                logits(0)
                logits(1)
                for u in range(len(units)):
                    probabilities(u)
                    if u + 2 < len(units):
                        logits(u + 2)

            @block.tensor
            def _(pe):
                mm, tr = nc.tensor.matmul, nc.tensor.transpose
                ident, ones = t.c(C_ID), t.c(C_ONES)
                for b in range(NB):
                    last = tr(t.bank[7][:, b * P:(b + 1) * P], proj[:, AB0, PAD + b * P:PAD + (b + 1) * P], ident)
                last.then_inc(s["w_t"], 1)

                def up_project(n):
                    j = order[n]
                    if n >= 4:
                        pe.wait_ge(s["up_out"], n - 3)
                    for c in range(2):
                        if j < QI0:
                            left, right = wq[:, c, j * P:(j + 1) * P], lat[:, c, :]
                        elif j < K0:
                            left, right = wqi[:, c, (j - QI0) * P:(j - QI0 + 1) * P], lat[:, c, :]
                        else:
                            left, right = wkv[:, c, 0, (j - K0) * P:(j - K0 + 1) * P], lat[:, 2 + c, :]
                        last = mm(t.bank[n % 4][:], left, right, start=c == 0, stop=c == 1)
                    last.then_inc(s["up"], 1)

                for n in range(IH // 2):
                    up_project(n)
                pe.wait_ge(s["rel"], 32)
                mm(t.bank[4][0:H, :], rel[:], buckets[:, 0:T], start=True, stop=True)
                mm(t.bank[5][0:H, 0:P], rel[:], buckets[:, T:W], start=True, stop=True).then_inc(s["strip"], 1)
                pe.wait_ge(s["up_out"], IH // 2)
                n = 0
                for b in range(1, NB):
                    S = (b + 1) * P
                    for i in range(IH):
                        if n >= 4:
                            pe.wait_ge(s["relu"], n - 3)
                        rows = slice(IDIM * (i % 2), IDIM * (i % 2) + IDIM)
                        mm(t.bank[n % 4][:, 0:S], up[rows, QI0 + i // 2, b * P:(b + 1) * P], kin[rows, 0:S],
                           start=True, stop=True).then_inc(s["dots"], 1)
                        n += 1
                pe.wait_ge(s["w"], 1)
                pe.wait_ge(s["slid"], 16 * H)
                for h in range(H):
                    if h >= 2:
                        pe.wait_ge(s["bias"], h - 1)
                    mm(t.bank[6 + h % 2][:], t.c(C_ANTI), slid[:, h, :], start=True, stop=True).then_inc(s["flip"], 1)
                pe.wait_ge(s["relu"], dots)
                pe.wait_ge(s["wq"], 16)
                pe.wait_ge(s["wkv"], 16)
                for n in range(IH // 2, NUP):
                    up_project(n)
                pe.wait_ge(s["strip_s"], 2)
                for b in range(NB):
                    if b >= 2:
                        pe.wait_ge(s["v_out"], b - 1)
                    for c in range(2):
                        last = mm(t.bank[4 + b % 2][:], lat[:, 2 + c, b * P:(b + 1) * P], wkv[:, c, 1, :],
                                  start=c == 0, stop=c == 1)
                    last.then_inc(s["v_up"], 1)
                pe.wait_ge(s["up_out"], NUP)
                pe.wait_ge(s["bias"], H)
                pe.wait_ge(s["v_out"], NB)

                def logits(u):
                    b, h = units[u]
                    if u >= 4:
                        pe.wait_ge(s["peak"], u - 3)
                    mm(t.bank[u % 4][:, 0:(b + 1) * P], up[:, h, b * P:(b + 1) * P], up[:, K0 + h, 0:(b + 1) * P],
                       start=True, stop=True).then_inc(s["logits"], 1)

                def values(u):
                    b, h = units[u]
                    pe.wait_ge(s["turned"], u + 1)
                    if u >= 2:
                        pe.wait_ge(s["mixed"], u - 1)
                    for k in range(b + 1):
                        last = mm(t.bank[6 + u % 2][:, 0:P], vt[:, k, h * P:(h + 1) * P], prt[:, u % 4, k * P:(k + 1) * P],
                                  start=k == 0, stop=k == b)
                    last.then_inc(s["pv"], 1)

                logits(0)
                logits(1)
                for u, (b, h) in enumerate(units):
                    if u + 2 < len(units):
                        logits(u + 2)
                    pe.wait_ge(s["prob"], u + 1)
                    if u >= 2:
                        pe.wait_ge(s["turned"], u - 1)
                    for k in range(b + 1):
                        last = tr(t.bank[4 + u % 2][:, k * P:(k + 1) * P], pr[:, u % 4, k * P:(k + 1) * P], ident)
                    last.then_inc(s["prob_t"], 1)
                    if u:
                        values(u - 1)
                values(len(units) - 1)


def route_stage(t, qy, hi, lo, u_d, keys_d, gates_d, active_d):
    nc = t.nc
    N = PK
    BODY, BODIES = (14, 16, 2), 4
    START = (0, 4 * 14, 4 * (14 + 16))
    TOK = 8
    ld_u = [t.sem(f"rt_u_loaded{i}") for i in range(2)]
    kept_a = [t.sem(f"rt_active_stored{i}") for i in range(2)]
    sent = [t.sem(f"rt_chunk_sent{i}") for i in range(2)]
    u_high, u_low, first, active = (t.sem("rt_" + k) for k in ("u_high", "u_low", "first", "active"))
    s = {n: t.sem("rt_" + n) for n in (
        "chain", "keys", "picked", "scores", "taken", "tops", "exps", "chosen", "slots_t", "slots", "gate_low",
        "hot", "hot2", "scaled", "placed", "low_out", "added")}
    with ExitStack() as ctx:
        def sb(name, shape, dt=F32):
            return ctx.enter_context(nc.sbuf_tensor("rt_" + name, shape, dt))

        u_raw, act_s = sb("u_raw", [P, 2, D]), sb("act", [P, 2, T])
        u_hi, u_lo = sb("u_hi", [P, 2, D], F32R), sb("u_lo", [P, 2, D], F32R)
        early = sb("early", [P, PK * CH])
        size = 2 * PH * P
        keys, qb = (early[:, k * size:(k + 1) * size].rearrange("p (a b) -> p a b", b=P) for k in range(2))
        hit = early[:, 2 * size:3 * size].rearrange("p (h a b) -> p h a b", h=PH, a=PTOP)
        val = sb("val", [P, 2, PTOP])
        num = sb("num", [P, 2, PH, PTOP], U32)
        pos, top = sb("pos", [P, PH, PTOP], U32), sb("top", [P, PH, PTOP])
        work = sb("work", [P, 2, PK])
        cand, cwork = sb("cand", [P, PTOP * PTOP]), sb("cwork", [P, PTOP * PTOP])
        part = sb("part", [P, 2, PH, PTOP], U32)
        part_f, num_f = sb("part_f", [P, 2, PH, PTOP]), sb("num_f", [P, 2, PH, PTOP])
        peak, total = sb("peak", [P, PH]), sb("total", [P, PH])
        out = sb("out", [P, 3, PH * PTOP])
        slot1, slot2, gate = sb("slot1", [P, T]), sb("slot2", [P, T]), sb("gate", [P, T])
        gate_hi, gate_lo = sb("gate_hi", [P, T], F32R), sb("gate_lo", [P, T])
        hot1, hot2 = sb("hot1", [P, 2, TOK, P], F32R), sb("hot2", [P, 2, TOK, P])
        gated = sb("gated", [P, 2, TOK, 2, P], F32R)
        low_part = sb("low_part", [P, TOK // 2, PK, 2])
        table = [ap.rearrange("p (e n) -> p e n", e=PK) for ap in (early[:], qy[:].rearrange("p a b -> p (a b)"))]

        def run(eng, slot):
            for phase in range(3):
                for j in range(BODY[phase]):
                    slot(phase, 0, j, True)
                with eng.Fori(1, BODIES) as i:
                    for j in range(BODY[phase]):
                        slot(phase, i, j, False)

        def number(phase, i, j):
            return START[phase] + BODY[phase] * i + j

        def turn(phase, i, j):
            return START[phase] // 2 + BODY[phase] // 2 * i + j // 2

        with nc.Block() as block:

            @block.sync
            def _(sp):
                sp.dma_start(keys, keys_d).then_inc(s["keys"], 16)

                def load(e, par, free):
                    if free:
                        sp.wait_ge(u_low, e - 1)
                    sp.dma_start(u_raw[:, par, :], u_d[e]).then_inc(ld_u[par], 16)

                def store(e, par):
                    sp.wait_ge(active, e + 1)
                    sp.dma_start(active_d[e], act_s[:, par, :]).then_inc(kept_a[par], 16)

                load(0, 0, False)
                load(1, 1, False)
                load(2, 0, True)
                load(3, 1, True)
                store(0, 0)
                with sp.Fori(2, N // 2) as i:
                    for par in range(2):
                        load(2 * i + par, par, True)
                        store(2 * i + par - 3, 1 - par)
                store(N - 3, 1)
                store(N - 2, 0)
                store(N - 1, 1)
                for par in range(2):
                    sp.wait_ge(kept_a[par], 16 * (N // 2))

            @block.scalar
            def _(act):
                a = nc.scalar.activation

                def gelu(e, par, uses):
                    act.wait_ge(first, e + 1)
                    if uses is not None:
                        act.wait_ge(kept_a[par], 16 * uses)
                    a(act_s[:, par, :], t.bank[par][:], ACT.Gelu).then_inc(active, 1)

                def send(i, j):
                    par, quarter = (j - 7) // 8 % 2, (j - 7) % 8
                    if quarter == 0:
                        act.wait_ge(s["added"], 4 * (BODY[1] * i + j + 1))
                    if quarter < 4:
                        chunk = 2 * i + (j - 7) // 8
                        rows = slice(quarter * PK // 4, (quarter + 1) * PK // 4)
                        act.dma_start(gates_d[:, bass.ds(chunk, 1), rows, :],
                                      table[par][:, rows, :]).then_inc(sent[par], 16)

                def slot(phase, i, j, head):
                    e = number(phase, i, j)
                    if phase == 0 and j == 0:
                        if not head:
                            act.wait_ge(s["scores"], PH * i)
                        a(qb, qy[:, :, bass.ds(i * P, P)], ACT.Copy).then_inc(s["picked"], 1)
                    if phase == 1 and (j >= 2 or not head) or phase == 2 and head:
                        step = e - START[1] - 2
                        for g in range(TOK // 2):
                            act.wait_ge(s["placed"], 4 * step + g + 1)
                            a(low_part[:, g], t.bank[2 + g][:].rearrange("p (n l e) -> p l e n", n=2, l=2)[:, 1],
                              ACT.Copy).then_inc(s["low_out"], 1)
                    act.wait_ge(ld_u[j % 2], 16 * (turn(phase, i, j) + 1))
                    fresh = head and phase == 0 and j < 2
                    if not fresh:
                        act.wait_ge(first, e - 1)
                    a(u_hi[:, j % 2, :], u_raw[:, j % 2, :], ACT.Copy).then_inc(u_high, 1)
                    if not fresh:
                        old = not (head and phase == 0 and j < 4)
                        gelu(e - 2, j % 2, turn(phase, i, j) - 1 if old else None)
                    if phase == 1:
                        step = BODY[1] * i + j
                        act.wait_ge(s["hot2"], step + 1)
                        for k in range(TOK):
                            last = a(gated[:, j % 2, k, 1, :], hot2[:, j % 2, k, :], ACT.Copy,
                                     scale=gate_lo[:, bass.ds(step * TOK + k, 1)])
                        last.then_inc(s["scaled"], 1)
                    if phase == 0 and j == BODY[0] - 1:
                        act.wait_ge(s["slots_t"], i + 1)
                        turned = t.bank[6]
                        cols = bass.ds(i * P, P)
                        a(slot1[:, cols], turned[:, 0:P], ACT.Copy)
                        a(slot2[:, cols], turned[:, P:2 * P], ACT.Copy)
                        a(gate[:, cols], turned[:, 2 * P:3 * P], ACT.Copy)
                        a(gate_hi[:, cols], turned[:, 2 * P:3 * P], ACT.Copy).then_inc(s["slots"], 1)
                    if phase == 0 and j == BODY[0] - 3:
                        act.wait_ge(s["tops"], i + 1)
                        a(top[:], top[:], ACT.Exp).then_inc(s["exps"], 1)
                    if phase == 1:
                        if j >= 2 and not (head and j < 9):
                            send(i, j - 2)
                        elif j < 2 and not head:
                            send(i - 1, BODY[1] + j - 2)
                    if phase == 2 and head:
                        send(BODIES - 1, BODY[1] + j - 2)
                        if j == 1:
                            for k in range(3):
                                send(BODIES - 1, BODY[1] + k)

                run(act, slot)
                gelu(N - 2, 0, N // 2 - 1)
                gelu(N - 1, 1, N // 2 - 1)
                for par in range(2):
                    act.wait_ge(sent[par], 16 * 4 * BODIES)

            @block.gpsimd
            def _(pool):
                def low(e, par):
                    pool.wait_ge(u_high, e + 1)
                    nc.gpsimd.tensor_tensor(u_lo[:, par, :], u_raw[:, par, :], u_hi[:, par, :].bitcast(F32),
                                            ALU.subtract).then_inc(u_low, 1)
                with pool.Fori(0, N // 2) as i:
                    for par in range(2):
                        low(2 * i + par, par)

            @block.vector
            def _(dve):
                d = nc.vector

                def chosen_block(i, head):
                    links = [0]
                    per = PH * 8 + 9

                    def link(ins):
                        links[0] += 1
                        ins.then_inc(s["chain"], 1)
                        dve.wait_ge(s["chain"], per * i + links[0])

                    for h in range(PH):
                        u = PH * i + h
                        dve.wait_ge(s["scores"], u + 1)
                        sc = [t.bank[2 + h % 4][:, side * PK:(side + 1) * PK] for side in range(2)]
                        d.max(val[:, 0, 0:8], sc[0])
                        link(d.max(val[:, 1, 0:8], sc[1]))
                        for side in range(2):
                            d.max_index(num[:, side, h, 0:8], val[:, side, 0:8], sc[side])
                            ins = d.match_replace(work[:, side, :], val[:, side, 0:8], sc[side], TAKEN)
                        ins.then_inc(s["taken"], 1)
                        dve.wait_ge(s["taken"], u + 1)
                        d.max(val[:, 0, 8:16], work[:, 0, :])
                        link(d.max(val[:, 1, 8:16], work[:, 1, :]))
                        for side in range(2):
                            d.max_index(num[:, side, h, 8:16], val[:, side, 8:16], work[:, side, :])
                        link(d.tensor_tensor(cand[:].rearrange("p (a b) -> p a b", a=PTOP),
                                             val[:, 0, :].unsqueeze(2).to_broadcast([P, PTOP, PTOP]),
                                             val[:, 1, :].unsqueeze(1).to_broadcast([P, PTOP, PTOP]), ALU.add))
                        link(d.max(top[:, h, 0:8], cand[:]))
                        d.max_index(pos[:, h, 0:8], top[:, h, 0:8], cand[:])
                        link(d.match_replace(cwork[:], top[:, h, 0:8], cand[:], TAKEN))
                        link(d.max(top[:, h, 8:16], cwork[:]))
                        link(d.max_index(pos[:, h, 8:16], top[:, h, 8:16], cwork[:]))
                        link(d.tensor_copy(peak[:, h:h + 1], top[:, h, 0:1]))
                    d.tensor_tensor(top[:], top[:], peak[:].unsqueeze(2).to_broadcast([P, PH, PTOP]),
                                    ALU.subtract).then_inc(s["tops"], 1)
                    d.tensor_scalar(part[:, 0], pos[:], 4, None, ALU.logical_shift_right)
                    link(d.tensor_scalar(part[:, 1], pos[:], PTOP - 1, None, ALU.bitwise_and))
                    d.tensor_copy(part_f[:], part[:])
                    link(d.tensor_copy(num_f[:], num[:]))
                    if not head:
                        dve.wait_ge(s["slots_t"], i)
                    iota = t.c(C_IOTA)[:, 0:PTOP].unsqueeze(1).unsqueeze(1).to_broadcast([P, PH, PTOP, PTOP])
                    for side in range(2):
                        link(d.tensor_tensor(hit, part_f[:, side].unsqueeze(3).to_broadcast([P, PH, PTOP, PTOP]),
                                             iota, ALU.is_equal))
                        link(d.tensor_tensor(hit, hit, num_f[:, side].unsqueeze(2).to_broadcast([P, PH, PTOP, PTOP]),
                                             ALU.mult))
                        ins = d.tensor_reduce(out[:, side, :].rearrange("p (h k) -> p h k", h=PH), hit, AX.X, ALU.add)
                        if side == 0:
                            link(ins)
                    dve.wait_ge(s["exps"], i + 1)
                    link(d.tensor_reduce(total[:], top[:], AX.X, ALU.add))
                    link(d.reciprocal(total[:], total[:]))
                    d.tensor_tensor(out[:, 2, :].rearrange("p (h k) -> p h k", h=PH), top[:],
                                    total[:].unsqueeze(2).to_broadcast([P, PH, PTOP]), ALU.mult).then_inc(s["chosen"], 1)
                    assert links[0] == per, links

                for i in range(NB):
                    chosen_block(i, i == 0)
                dve.wait_ge(s["slots"], NB)
                d.tensor_tensor(gate_lo[:], gate[:], gate_hi[:].bitcast(F32), ALU.subtract).then_inc(s["gate_low"], 1)
                dve.wait_ge(s["gate_low"], 1)
                iota = t.c(C_IOTA)

                def hots(i, j, head):
                    step = BODY[1] * i + j
                    cols = bass.ds(step * TOK, TOK)

                    def wide(ap):
                        return ap[:, cols].unsqueeze(2).to_broadcast([P, TOK, P])
                    keys_row = iota.unsqueeze(1).to_broadcast([P, TOK, P])
                    if not (head and j < 2):
                        dve.wait_ge(s["placed"], 4 * (step - 1))
                    d.tensor_tensor(hot2[:, j % 2], keys_row, wide(slot2), ALU.is_equal).then_inc(s["hot2"], 1)
                    d.tensor_tensor(hot1[:, j % 2], keys_row, wide(slot1), ALU.is_equal)
                    dve.wait_ge(s["hot2"], step + 1)
                    d.tensor_tensor(gated[:, j % 2, :, 0, :], hot2[:, j % 2], wide(gate_hi[:].bitcast(F32)),
                                    ALU.mult).then_inc(s["hot"], 1)

                def add_up(i, j, head):
                    par, local = j // 8, j % 8
                    if local == 0 and not head:
                        dve.wait_ge(sent[par], 16 * 4 * i)
                    for g in range(TOK // 2):
                        dve.wait_ge(s["low_out"], 4 * (BODY[1] * i + j) + g + 1)
                        parts = t.bank[2 + g][:].rearrange("p (n l e) -> p l e n", n=2, l=2)
                        at = local * TOK + 2 * g
                        d.tensor_tensor(table[par][:, :, at:at + 2], parts[:, 0], low_part[:, g],
                                        ALU.add).then_inc(s["added"], 1)

                for j in range(BODY[1]):
                    hots(0, j, True)
                    if j:
                        add_up(0, j - 1, True)
                with dve.Fori(1, BODIES) as i:
                    for j in range(BODY[1]):
                        hots(i, j, False)
                        if j:
                            add_up(i, j - 1, False)
                        else:
                            add_up(i - 1, BODY[1] - 1, False)
                add_up(BODIES - 1, BODY[1] - 1, False)

            @block.tensor
            def _(pe):
                mm = nc.tensor.matmul
                pe.wait_ge(s["keys"], 16)

                def slot(phase, i, j, head):
                    e = number(phase, i, j)
                    if phase == 0 and j < PH:
                        h = j
                        if j == 0:
                            pe.wait_ge(s["picked"], i + 1)
                        if not (head and h < 4):
                            pe.wait_ge(s["taken"], PH * i + h - 3)
                        for side in range(2):
                            last = mm(t.bank[2 + h % 4][:, side * PK:(side + 1) * PK], qb[:, 2 * h + side, :],
                                      keys[:, 2 * h + side, :], start=True, stop=True)
                        last.then_inc(s["scores"], 1)
                    if phase == 0 and j == BODY[0] - 1:
                        pe.wait_ge(s["chosen"], i + 1)
                        if not head:
                            pe.wait_ge(s["slots"], i)
                        for k in range(3):
                            last = nc.tensor.transpose(t.bank[6][:, k * P:(k + 1) * P], out[:, k, :], t.c(C_ID))
                        last.then_inc(s["slots_t"], 1)
                    pe.wait_ge(u_low, e + 1)
                    if not (head and phase == 0 and j < 2):
                        pe.wait_ge(active, e - 1)
                    bank = t.bank[j % 2][:]
                    for c in range(DC):
                        cols = slice(c * P, (c + 1) * P)
                        mm(bank, u_hi[:, j % 2, cols], hi[:, c, :], start=c == 0, stop=False)
                        mm(bank, u_hi[:, j % 2, cols], lo[:, c, :], start=False, stop=False)
                        last = mm(bank, u_lo[:, j % 2, cols], hi[:, c, :], start=False, stop=c == DC - 1)
                    last.then_inc(first, 1)
                    if phase == 1:
                        step = BODY[1] * i + j
                        pe.wait_ge(s["hot"], step + 1)
                        pe.wait_ge(s["scaled"], step + 1)
                        for g in range(TOK // 2):
                            if not (head and j == 0):
                                pe.wait_ge(s["added"], 4 * step + g - 3)
                            for k in range(2):
                                tok = 2 * g + k
                                last = mm(t.bank[2 + g][:, 2 * k * P:2 * (k + 1) * P], hot1[:, j % 2, tok, :],
                                          gated[:, j % 2, tok], start=True, stop=True)
                            last.then_inc(s["placed"], 1)
                run(pe, slot)


def value_stage(t, v_d, gates_d, active_d):
    nc = t.nc
    N = PK

    ld_v, ld_w, ld_g = ([t.sem(f"va_{k}_loaded{i}") for i in range(2)] for k in ("v", "w", "gates"))
    v_high, v_low, gated, w_high, w_low, second = (
        t.sem("va_" + k) for k in ("v_high", "v_low", "gated", "w_high", "w_low", "second"))
    with ExitStack() as ctx:
        def sb(name, shape, dt=F32):
            return ctx.enter_context(nc.sbuf_tensor("va_" + name, shape, dt))

        v_raw = sb("v_raw", [P, 2, D])
        v_hi, v_lo = sb("v_hi", [P, 2, D], F32R), sb("v_lo", [P, 2, D], F32R)
        gate = sb("gate", [P, 2, T // CH, 2, CH])
        act_s, w = sb("act", [P, 2, T]), sb("w", [P, 2, T])
        w_hi, w_lo = sb("w_hi", [P, 2, T], F32R), sb("w_lo", [P, 2, T], F32R)

        def run(eng, slot, n=N // 2):
            slot(0, 0, True)
            slot(0, 1, True)
            with eng.Fori(1, n // 2) as i:
                slot(i, 0, False)
                slot(i, 1, False)

        with nc.Block() as block:

            @block.sync
            def _(sp):
                def pair(i, q, head):
                    u = 2 * i + q
                    if not head:
                        sp.wait_ge(gated, 2 * u - 2)
                    sp.dma_start(gate[:, q], gates_d[:, :, bass.ds(2 * u, 2), :]).then_inc(ld_g[q], 16)
                    for j in range(2):
                        e = 2 * u + j
                        if not (head and q == 0):
                            sp.wait_ge(v_low, e - 1)
                        sp.dma_start(v_raw[:, j, :], v_d[:, e, :]).then_inc(ld_v[j], 16)
                        if not (head and q == 0):
                            sp.wait_ge(gated, e - 1)
                        sp.dma_start(act_s[:, j, :], active_d[e]).then_inc(ld_w[j], 16)
                run(sp, pair)

            @block.scalar
            def _(act):
                def pair(i, q, head):
                    u = 2 * i + q
                    for j in range(2):
                        e = 2 * u + j
                        act.wait_ge(ld_v[j], 16 * (u + 1))
                        if not (head and q == 0):
                            act.wait_ge(second, e - 1)
                        nc.scalar.activation(v_hi[:, j, :], v_raw[:, j, :], ACT.Copy).then_inc(v_high, 1)
                        act.wait_ge(gated, e + 1)
                        nc.scalar.activation(w_hi[:, j, :], w[:, j, :], ACT.Copy).then_inc(w_high, 1)
                run(act, pair)

            @block.vector
            def _(dve):
                def minus(out, a, high, done):
                    nc.vector.tensor_tensor(out, a, high.bitcast(F32), ALU.subtract).then_inc(done, 1)

                def pair(i, q, head):
                    u = 2 * i + q
                    dve.wait_ge(ld_g[q], 16 * (i + 1))
                    for j in range(2):
                        e = 2 * u + j
                        dve.wait_ge(ld_w[j], 16 * (u + 1))
                        chunks = [ap[:, j, :].rearrange("p (c n) -> p c n", n=CH) for ap in (w, act_s)]
                        nc.vector.tensor_tensor(chunks[0], chunks[1], gate[:, q, :, j, :], ALU.mult).then_inc(gated, 1)
                        dve.wait_ge(v_high, e + 1)
                        minus(v_lo[:, j, :], v_raw[:, j, :], v_hi[:, j, :], v_low)
                        dve.wait_ge(w_high, e + 1)
                        minus(w_lo[:, j, :], w[:, j, :], w_hi[:, j, :], w_low)
                run(dve, pair)

            @block.tensor
            def _(pe):
                mm = nc.tensor.matmul

                def slot(i, j, start=False, stop=False):
                    e = 2 * i + j
                    pe.wait_ge(v_low, e + 1)
                    pe.wait_ge(w_low, e + 1)
                    for d in range(DC):
                        bank, cols = t.bank[d][:], slice(d * P, (d + 1) * P)
                        mm(bank, v_hi[:, j, cols], w_hi[:, j, :], start=start, stop=False)
                        mm(bank, v_hi[:, j, cols], w_lo[:, j, :], start=False, stop=False)
                        last = mm(bank, v_lo[:, j, cols], w_hi[:, j, :], start=False, stop=stop)
                    last.then_inc(second, 1)

                slot(0, 0, start=True)
                slot(0, 1)
                with pe.Fori(1, N // 2 - 1) as i:
                    slot(i, 0)
                    slot(i, 1)
                slot(N // 2 - 1, 0)
                slot(N // 2 - 1, 1, stop=True)


def final_stage(t, x, gain, out_d):
    nc = t.nc
    added, squared, summed, logged, inverted, normed, stored = (
        t.sem(f"final_{n}") for n in ("added", "squared", "summed", "logged", "inverted", "normed", "stored"))
    with ExitStack() as ctx:
        sq = ctx.enter_context(nc.sbuf_tensor("final_sq", [P, DC, T], F32))
        y = ctx.enter_context(nc.sbuf_tensor("final_y", [P, DC, T], F32))
        log = ctx.enter_context(nc.sbuf_tensor("final_log", [P, T], F32))
        inv = ctx.enter_context(nc.sbuf_tensor("final_inv", [P, T], F32))
        with nc.Block() as block:

            @block.sync
            def _(sp):
                for c in range(DC):
                    sp.wait_ge(normed, c + 1)
                    sp.dma_start(out_d[:, c, :], y[:, c, :]).then_inc(stored, 16)
                sp.wait_ge(stored, 16 * DC)

            @block.scalar
            def _(act):
                a = nc.scalar.activation
                for c in range(DC):
                    act.wait_ge(added, c + 1)
                    a(sq[:, c, :], x[:, c, :], ACT.Square).then_inc(squared, 1)
                act.wait_ge(summed, 1)
                a(log[:], t.bank[0][:], ACT.Ln, scale=1.0 / D, bias=t.vec[:, V_EPS:V_EPS + 1]).then_inc(logged, 1)
                act.wait_ge(logged, 1)
                a(inv[:], log[:], ACT.Exp, scale=-0.5).then_inc(inverted, 1)

            @block.tensor
            def _(pe):
                for c in range(DC):
                    pe.wait_ge(squared, c + 1)
                    last = nc.tensor.matmul(t.bank[0][:], t.c(C_ONES), sq[:, c, :],
                                            start=c == 0, stop=c == DC - 1)
                last.then_inc(summed, 1)

            @block.vector
            def _(dve):
                for c in range(DC):
                    nc.vector.tensor_tensor(x[:, c, :], x[:, c, :], t.bank[c][:], ALU.add).then_inc(added, 1)
                dve.wait_ge(added, DC)
                dve.wait_ge(inverted, 1)
                for c in range(DC):
                    nc.vector.scalar_tensor_tensor(y[:, c, :], x[:, c, :], t.vec[:, gain + c:gain + c + 1],
                                                   inv[:], ALU.mult, ALU.mult).then_inc(normed, 1)


def build(nc, a):
    with ExitStack() as outer:
        t = Tables(nc, outer)
        x = outer.enter_context(nc.sbuf_tensor("x_stream", [P, DC, T], F32))
        with ExitStack() as mixers:
            mix = mixers.enter_context(nc.sbuf_tensor("mix", [P, 2 * H, T], F32))
            with ExitStack() as inner:
                proj = inner.enter_context(nc.sbuf_tensor("proj", [P, NPROJ, PAD + T + 1], F32))
                wqi = inner.enter_context(nc.sbuf_tensor("w_qidx", [P, 2, IH * IDIM], F32))
                with ExitStack() as gdn:
                    conv = gdn.enter_context(nc.sbuf_tensor("conv", [P, QKV_T, T], F32))
                    zeroed = t.sem("pad_zeroed")
                    with nc.Block() as block:

                        @block.vector
                        def _(dve):
                            nc.vector.memset(proj[:, :, 0:PAD], 0.0).then_inc(zeroed, 1)
                    with ExitStack() as split:
                        hi = split.enter_context(nc.sbuf_tensor("h1_hi", [P, DC, T], F32R))
                        lo = split.enter_context(nc.sbuf_tensor("h1_lo", [P, DC, T], F32R))
                        h1 = split.enter_context(nc.sbuf_tensor("h1", [P, DC, T], F32))
                        conv_root = split.enter_context(nc.sbuf_tensor("conv_root", [P, 2, T], F32))
                        project_stage(t, "in", a["w_in"], NPROJ, x, V_LN1, hi, lo, lambda i: proj[:, i, PAD:PAD + T],
                                      side=convolution(t, proj, conv, h1, conv_root), y=h1, fetch=(a["x"], a["constants"], a["vectors"]))
                    delta_stage(t, proj, conv, mix, wqi, a["w_qidx_up"])
                sparse_stage(t, proj, mix, wqi, a["w_q_up"], a["w_kv_up"], a["rel_bias"],
                             a["buckets"], a["strip"])
            with ExitStack() as split:
                hi = split.enter_context(nc.sbuf_tensor("mix_hi", [P, DC, T], F32R))
                lo = split.enter_context(nc.sbuf_tensor("mix_lo", [P, DC, T], F32R))
                project_stage(t, "out", a["w_out"], DC, mix, None, hi, lo, lambda i: x[:, i, :],
                              add=lambda i: x[:, i, :])
        t.free_semaphores()
        with ExitStack() as peer:
            hi = peer.enter_context(nc.sbuf_tensor("h2_hi", [P, DC, T], F32R))
            lo = peer.enter_context(nc.sbuf_tensor("h2_lo", [P, DC, T], F32R))
            with ExitStack() as route:
                qy = route.enter_context(nc.sbuf_tensor("qy", [P, 2 * PH, T], F32))
                project_stage(t, "query", a["w_query"], 2 * PH, x, V_LN2, hi, lo, lambda i: qy[:, i, :])
                route_stage(t, qy, hi, lo, a["u"], a["keys"], a["gates"], a["active"])
        value_stage(t, a["v"], a["gates"], a["active"])
        final_stage(t, x, V_FIN, a["out"])


def tiles(w, n):
    return np.ascontiguousarray(w.reshape(DC, P, n, P).transpose(2, 1, 0, 3)).reshape(n, P, D)


def layout(inputs):
    f = {k: np.asarray(v) for k, v in inputs.items()}
    w_in = f["w_in"][0]
    ab = 4 * H * P
    rest = ab + 2 * H
    idx = rest + 2 * RANK
    cols = [w_in[:, 0:ab], w_in[:, rest:idx], w_in[:, idx:idx + IDIM], w_in[:, idx:idx + IDIM],
            w_in[:, ab:rest], w_in[:, idx + IDIM:], np.zeros((D, P - 2 * H - IH), np.float32)]
    vec = np.zeros((P, V_N), np.float32)
    vec[:, V_LN1:V_LN1 + DC] = f["ln1_g"][0].reshape(DC, P).T
    vec[:, V_LN2:V_LN2 + DC] = f["ln2_g"][0].reshape(DC, P).T
    vec[:, V_FIN:V_FIN + DC] = f["final_g"].reshape(DC, P).T
    vec[:, V_CONV:V_CONV + 3 * H * CONV] = f["conv_w"][0].reshape(CONV, 3 * H, P).transpose(2, 1, 0).reshape(P, -1)
    vec[:, V_GDN] = f["gdn_norm_g"][0]
    vec[:, V_QN:V_QN + 2] = f["q_norm_g"][0].reshape(2, P).T
    vec[:, V_KVN:V_KVN + 2] = f["kv_norm_g"][0].reshape(2, P).T
    vec[:, V_IG] = np.concatenate([f["idx_ln_g"][0]] * 2)
    vec[:, V_IB] = np.concatenate([f["idx_ln_b"][0]] * 2)
    vec[:, V_EPS] = EPS
    vec[:, V_ALOG:V_ALOG + H] = f["a_log"][0]
    vec[:, V_DTB:V_DTB + H] = f["dt_bias"][0]
    vec[:, V_QK:V_QK + H] = P ** -0.5
    vec[:, V_QK + H:V_QK + 2 * H] = 1.0
    keys = np.stack([f["peer_sub_keys_1"][0], f["peer_sub_keys_2"][0]], axis=1)
    return {
        "x": np.ascontiguousarray(f["x"][0].T.reshape(DC, P, T).transpose(1, 0, 2)),
        "constants": constants(), "vectors": vec, "buckets": bucket_rows(),
        "w_in": tiles(np.concatenate(cols, axis=1), NPROJ),
        "w_q_up": np.ascontiguousarray(f["w_q_up"][0].reshape(2, P, -1).transpose(1, 0, 2)),
        "w_qidx_up": np.ascontiguousarray(f["w_qidx_up"][0].reshape(2, P, -1).transpose(1, 0, 2)),
        "w_kv_up": np.ascontiguousarray(f["w_kv_up"][0].reshape(2, P, H, 2, P).transpose(1, 0, 3, 2, 4)).reshape(P, 2, 2, H * P),
        "rel_bias": f["rel_bias"],
        "w_out": tiles(f["w_out"][0], DC),
        "w_query": tiles(f["peer_w_query"][0], 2 * PH),
        "keys": np.ascontiguousarray(keys.reshape(2 * PH, PK, P).transpose(2, 0, 1)),
        "u": np.ascontiguousarray(f["peer_u"][0].reshape(PK, PK, DC, P).transpose(1, 3, 2, 0)).reshape(PK, P, D),
        "v": f["peer_v"][0].reshape(PK, PK, D),
    }


def kernel(**inputs):
    import concourse.bacc as bacc
    from concourse.bass_utils import run_bass_kernel_spmd

    nc = bacc.Bacc("TRN2", target_bir_lowering=False, num_devices=1)
    arrays = layout(inputs)
    a = {k: nc.dram_tensor(k + "_dram", v.shape, F32, kind="ExternalInput").ap() for k, v in arrays.items()}
    a["out"] = nc.dram_tensor("out_dram", (P, DC, T), F32, kind="ExternalOutput").ap()
    a["strip"] = nc.dram_tensor("strip_scratch", (H, T + P), F32).ap()
    a["active"] = nc.dram_tensor("active_scratch", (PK, P, T), F32).ap()
    a["gates"] = nc.dram_tensor("gates_scratch", (P, T // CH, PK, CH), F32).ap()
    build(nc, a)
    r = run_bass_kernel_spmd(nc, [{k + "_dram": v for k, v in arrays.items()}], core_ids=[0])
    out = r.results[0]["out_dram"]
    return np.ascontiguousarray(out.transpose(1, 0, 2).reshape(D, T).T).reshape(1, T, D)
```
